# Optimizing a Trainium2 kernel written in Bass

```python
import math
import jax, jax.numpy as jnp
from jax import lax
import numpy as np

D_MODEL = 2048
BATCH = 1
SEQ = 256
DEPTH = 2

N_MIXERS = 2
N_HEADS = 16
Q_LORA = 512
KV_LORA = 512
QK_NOPE = 128
QK_ROPE = 64
V_HEAD = 128
QK_HEAD = QK_NOPE + QK_ROPE
ROPE_THETA = 10000.0
Q_BLOCK = 128
POOL_WINDOWS = (2, 4, 8, 16)
N_POOL_GROUPS = len(POOL_WINDOWS)
POOL_GROUP = D_MODEL // N_POOL_GROUPS
D_FF = 4 * D_MODEL
EPS = 1e-6
N_ATTN_LAYERS = (DEPTH + 1) // 2
N_POOL_LAYERS = DEPTH // 2

kernel_name = "hybrid_mla_multiscale_pool_sqrelu"

def rmsnorm(x, g):
    x32 = x.astype(jnp.float32)
    y = x32 * lax.rsqrt(jnp.mean(x32 * x32, axis=-1, keepdims=True) + EPS)
    return (y * g.astype(jnp.float32)).astype(x.dtype)

def rope_tables(positions):
    inv_freq = 1.0 / (ROPE_THETA ** (jnp.arange(0, QK_ROPE, 2, dtype=jnp.float32) / QK_ROPE))
    ang = positions.astype(jnp.float32)[..., None] * inv_freq
    return jnp.cos(ang), jnp.sin(ang)

def apply_rope(x, cos, sin):
    x32 = x.astype(jnp.float32)
    x1, x2 = jnp.split(x32, 2, axis=-1)
    out = jnp.concatenate([x1 * cos - x2 * sin, x2 * cos + x1 * sin], axis=-1)
    return out.astype(x.dtype)

def latent_attention(x, positions, w_dqkv, q_norm, kv_norm, w_uq, w_ukv, w_o):
    B, S, _ = x.shape
    c = x @ w_dqkv
    c_q = rmsnorm(c[..., :Q_LORA], q_norm)
    c_kv = rmsnorm(c[..., Q_LORA:Q_LORA + KV_LORA], kv_norm)
    k_rope = c[..., Q_LORA + KV_LORA:][:, :, None, :]

    q = (c_q @ w_uq).reshape(B, S, N_HEADS, QK_HEAD)
    kv = (c_kv @ w_ukv).reshape(B, S, N_HEADS, QK_NOPE + V_HEAD)
    k_nope, v = kv[..., :QK_NOPE], kv[..., QK_NOPE:]

    cos, sin = rope_tables(positions)
    cos, sin = cos[:, :, None, :], sin[:, :, None, :]
    q = jnp.concatenate([q[..., :QK_NOPE], apply_rope(q[..., QK_NOPE:], cos, sin)], axis=-1)
    k_rope = apply_rope(k_rope, cos, sin)
    k = jnp.concatenate([k_nope, jnp.broadcast_to(k_rope, (B, S, N_HEADS, QK_ROPE))], axis=-1)

    scale = 1.0 / math.sqrt(QK_HEAD)
    n_blocks = S // Q_BLOCK
    q_blocks = q.reshape(B, n_blocks, Q_BLOCK, N_HEADS, QK_HEAD).transpose(1, 0, 2, 3, 4)
    key_pos = jnp.arange(S)

    def attend(args):
        qb, bi = args
        s = jnp.einsum('bqhd,bkhd->bhqk', qb, k).astype(jnp.float32) * scale
        q_pos = bi * Q_BLOCK + jnp.arange(Q_BLOCK)
        mask = key_pos[None, :] <= q_pos[:, None]
        s = jnp.where(mask[None, None], s, -jnp.inf)
        p = jax.nn.softmax(s, axis=-1).astype(v.dtype)
        return jnp.einsum('bhqk,bkhd->bqhd', p, v)

    o = lax.map(attend, (q_blocks, jnp.arange(n_blocks)))
    o = o.transpose(1, 0, 2, 3, 4).reshape(B, S, N_HEADS * V_HEAD)
    return o @ w_o

def multiscale_pool(x, w_pool, pool_scale):
    B, S, D = x.shape
    xg = x.astype(jnp.float32).reshape(B, S, N_POOL_GROUPS, POOL_GROUP)
    cs = jnp.cumsum(xg, axis=1)
    t = jnp.arange(S)
    pooled = []
    for g, w in enumerate(POOL_WINDOWS):
        csg = cs[:, :, g]
        prev = jnp.pad(csg, ((0, 0), (w, 0), (0, 0)))[:, :S]
        cnt = jnp.minimum(t + 1, w).astype(jnp.float32)[None, :, None]
        pooled.append((csg - prev) / cnt)
    y = (jnp.stack(pooled, axis=2) - xg).astype(x.dtype)
    y = jnp.einsum('bsgc,gcd->bsgd', y, w_pool).reshape(B, S, D)
    return y * pool_scale

def sqrelu_mlp(x, w_up, w_down):
    h = jax.nn.relu(x @ w_up)
    return (h * h) @ w_down

def setup_inputs(seed: int = 0) -> dict:
    key = jax.random.key(seed)
    ks = jax.random.split(key, 16)
    f32 = jnp.float32

    def nrm(k, shape, fan_in):
        return jax.random.normal(k, shape, f32) * (fan_in ** -0.5)

    def gain(k, shape):
        return 1.0 + 0.05 * jax.random.normal(k, shape, f32)

    na, nb, nl = N_ATTN_LAYERS, N_POOL_LAYERS, DEPTH
    return {
        "x": jax.random.normal(ks[0], (BATCH, SEQ, D_MODEL), f32),
        "positions": jnp.broadcast_to(jnp.arange(SEQ, dtype=jnp.int32), (BATCH, SEQ)),
        "ln_mix": gain(ks[1], (nl, D_MODEL)),
        "ln_mlp": gain(ks[2], (nl, D_MODEL)),
        "w_dqkv": nrm(ks[3], (na, D_MODEL, Q_LORA + KV_LORA + QK_ROPE), D_MODEL),
        "q_norm": gain(ks[4], (na, Q_LORA)),
        "kv_norm": gain(ks[5], (na, KV_LORA)),
        "w_uq": nrm(ks[6], (na, Q_LORA, N_HEADS * QK_HEAD), Q_LORA),
        "w_ukv": nrm(ks[7], (na, KV_LORA, N_HEADS * (QK_NOPE + V_HEAD)), KV_LORA),
        "w_o": nrm(ks[8], (na, N_HEADS * V_HEAD, D_MODEL), N_HEADS * V_HEAD),
        "w_pool": nrm(ks[9], (nb, N_POOL_GROUPS, POOL_GROUP, POOL_GROUP), POOL_GROUP),
        "pool_scale": gain(ks[10], (nb, D_MODEL)),
        "w_up": nrm(ks[11], (nl, D_MODEL, D_FF), D_MODEL),
        "w_down": nrm(ks[12], (nl, D_FF, D_MODEL), D_FF),
        "final_norm": gain(ks[13], (D_MODEL,)),
    }

def reference(x, positions, ln_mix, ln_mlp, w_dqkv, q_norm, kv_norm, w_uq, w_ukv, w_o,
              w_pool, pool_scale, w_up, w_down, final_norm):
    h = x
    for i in range(DEPTH):
        hn = rmsnorm(h, ln_mix[i])
        j = i // N_MIXERS
        if i % N_MIXERS == 0:
            mix = latent_attention(hn, positions, w_dqkv[j], q_norm[j], kv_norm[j],
                                   w_uq[j], w_ukv[j], w_o[j])
        else:
            mix = multiscale_pool(hn, w_pool[j], pool_scale[j])
        h = h + mix
        h = h + sqrelu_mlp(rmsnorm(h, ln_mlp[i]), w_up[i], w_down[i])
    return rmsnorm(h, final_norm)


_drawn_inputs = setup_inputs


def setup_inputs(seed=0):
    import zlib

    import numpy as np

    out = dict(_drawn_inputs(seed))
    spreads = {}
    factors = {'q_norm': 5.788, 'kv_norm': 3.883, 'pool_scale': 5.312}
    for name, (base, spread) in spreads.items():
        noise = np.random.default_rng([zlib.crc32(name.encode()), seed]).standard_normal(out[name].shape)
        drawn = base * np.exp(spread * noise) if base else spread * noise
        out[name] = __import__('jax').numpy.asarray(drawn.astype(out[name].dtype))
    for name, factor in factors.items():
        out[name] = (out[name] * factor).astype(out[name].dtype)
    return out
```

```python
import math
from contextlib import ExitStack

import numpy as np

import concourse.bass as bass
from concourse import mybir

F32 = mybir.dt.float32
F32R = mybir.dt.float32r
I32 = mybir.dt.int32
ALU = mybir.AluOpType
ACT = mybir.ActivationFunctionType

P = 128
D_MODEL = 2048
SEQ = 256
NT = SEQ // P
KT = D_MODEL // P
N_HEADS = 16
LORA = 512
LT = LORA // P
NOPE = 128
ROPE = 64
HALF = ROPE // 2
QK_HEAD = NOPE + ROPE
V_HEAD = 128
GH = 4
GROUPS = N_HEADS // GH
ROPE_THETA = 10000.0
WINDOWS = (2, 4, 8, 16)
D_FF = 4 * D_MODEL
EPS = 1e-6
SCALE = 1.0 / math.sqrt(QK_HEAD)
MASKED = -3.0e38

COLS = 512
RAW_SLOTS = 4
LEAD = 4
SLABS = D_MODEL // COLS
FF_SLABS = D_FF // COLS
FB = COLS // P

U_DQKV = 0
U_ATT = U_DQKV + 2 * KT // 2
U_WO = U_ATT + 8 * GROUPS
U_MLP = (U_WO + SLABS * KT // 2, 0)
U_POOL = U_MLP[0] + 16 * FF_SLABS
U_MLP = (U_MLP[0], U_POOL + 2 * SLABS)
U_END = U_MLP[1] + 16 * FF_SLABS

S_WO = 0
S_MLP = (SLABS, SLABS + FF_SLABS * SLABS + SLABS)
S_POOL = S_MLP[0] + FF_SLABS * SLABS

S_END = S_MLP[1] + FF_SLABS * SLABS
SCORE_COLS = ((0, P), (P, 3 * P))

GAIN_COL = (0, 2 * KT, KT, 3 * KT)
Q_GAIN = 4 * KT
N_GAINS = 4 * KT + 2 * LT

TWO_PI_A = 6.28125
TWO_PI_B = float(np.float32(2 * math.pi - TWO_PI_A))
TWO_PI_B = float(np.float32(np.round(TWO_PI_B * 2**20) / 2**20))
TWO_PI_C = float(np.float32(2 * math.pi - TWO_PI_A - TWO_PI_B))
PI_IN = 3.1415925
ROUNDER = 1.5 * 2.0**23


def trunk(nc, x, positions, ln_mix, ln_mlp, w_dqkv, q_norm, kv_norm, w_uq, w_ukv, w_o,
          w_pool, pool_scale, w_up, w_down, final_norm, shape_consts, band_consts, out):
    ctx = ExitStack()
    with ctx:
        def sb(name, shape, dt=F32):
            return ctx.enter_context(nc.sbuf_tensor(name, shape, dt))

        def sem(name):
            return ctx.enter_context(nc.semaphore(name))

        resid = sb("resid", [P, NT, D_MODEL])
        weight_raw = sb("weight_raw", [P, RAW_SLOTS, 4, COLS])
        weight_hi = sb("weight_hi", [P, LEAD, 2, COLS], F32R)
        weight_lo = sb("weight_lo", [P, LEAD, 2, COLS], F32R)
        xt = sb("xt", [P, KT, 2 * SEQ], F32R)
        mid = sb("mid", [P, 2, FB, 2 * SEQ], F32R)
        scratch = sb("scratch", [P, 2 * D_MODEL])
        row_gain = sb("row_gain", [P, D_MODEL])
        early = sb("early", [P, 1536])
        q_t = sb("q_t", [P, GH, 2 * SEQ], F32R)
        k_t = sb("k_t", [P, GH, 2 * SEQ], F32R)
        v_hi = sb("v_hi", [P, NT, GH * V_HEAD], F32R)
        v_lo = sb("v_lo", [P, NT, GH * V_HEAD], F32R)
        qr_t = sb("qr_t", [P, 2, 2 * SEQ], F32R)
        kr_t = sb("kr_t", [P, 2, 2 * SEQ], F32R)
        p_t = sb("p_t", [P, GH, 6 * P], F32R)
        cos_t = sb("cos_t", [P, 2, SEQ])
        sin_t = sb("sin_t", [P, 2, SEQ])
        consts = sb("consts", [P, 3 * P + 1])
        gain_col = sb("gain_col", [P, N_GAINS])
        small = sb("small", [P, 96])
        ps = ctx.enter_context(nc.psum_tensor("ps", [P, 8, COLS], F32))

        ident = consts[:, 0:P]
        causal = consts[:, P:3 * P]
        inv_freq = consts[:, 3 * P:3 * P + 1]
        latent_t = mid[:, :, :, :].rearrange("p a b c -> p (a b) c")
        scaled = scratch[:, :].rearrange("p (t n) -> p t n", t=NT)
        latent = scratch[:, 0:2 * NT * LORA].rearrange("p (t n) -> p t n", t=NT)
        tail_raw = early[:, 0:KT * ROPE].rearrange("p (k c) -> p k c", k=KT)
        tail_hi = q_t[:, 0:2, :].rearrange("p a (k c) -> p (a k) c", c=ROPE)
        tail_lo = q_t[:, 2:4, :].rearrange("p a (k c) -> p (a k) c", c=ROPE)
        k_rope = early[:, KT * ROPE:KT * ROPE + 512].rearrange("p (t a r j) -> p t a r j", t=NT, a=2, r=4)
        probs = early[:, :].rearrange("p (h c) -> p h c", h=GH)
        band = early[:, :]
        gain_rows = early[0:N_GAINS, 11 * P:12 * P]
        fold_b = [scratch[:, s * 1024:(s + 1) * 1024].rearrange("p (b n) -> p b n", b=FB) for s in (0, 1)]
        fold_s = [scratch[:, s * 1024:(s + 1) * 1024].rearrange("p (b n) -> p b n", b=FB) for s in (2, 3)]
        rot_b = scratch[:, 1024:1536].rearrange("p (a n) -> p a n", a=2)
        rot_x = scratch[:, 1536:2048].rearrange("p (a n) -> p a n", a=2)
        rot_c = scratch[:, 3072:3584].rearrange("p (a n) -> p a n", a=2)
        rot_s = scratch[:, 3584:4096].rearrange("p (a n) -> p a n", a=2)
        pos_i = early[:, 8 * P:8 * P + SEQ].bitcast(I32)
        sumsq = small[:, 0:2]
        rstd = small[:, 2:4]
        root = small[:, 4:6]
        eps = small[:, 6:7]
        c_sumsq = small[:, 8:12].rearrange("p (j t) -> p j t", j=2)
        c_root = small[:, 12:16].rearrange("p (j t) -> p j t", j=2)
        c_rstd = small[:, 16:20].rearrange("p (j t) -> p j t", j=2)
        row_max = small[:, 24:32]
        neg_max = small[:, 32:40]
        row_sum = small[:, 40:48]
        inv_sum = small[:, 48:56]
        step_mark = small[:, 56:58]

        x_in = [sem(f"x_in{t}") for t in range(NT)]
        consts_in, gains_in, pos_in, tail_in = sem("consts_in"), sem("gains_in"), sem("pos_in"), sem("tail_in")
        band_in, scale_in, final_in, out_done = sem("band_in"), sem("scale_in"), sem("final_in"), sem("out_done")
        raw_in = [sem(f"raw_in{s}") for s in range(RAW_SLOTS)]
        hi_made, lo_made, unit_used = sem("hi_made"), sem("lo_made"), sem("unit_used")
        gains_turned, gains_ready, eps_set = sem("gains_turned"), sem("gains_ready"), sem("eps_set")
        squared_t0, squared_t1 = sem("squared_t0"), sem("squared_t1")
        rooted, rstd_made = sem("rooted"), sem("rstd_made")
        scaled_t0, scaled_t1 = sem("scaled_t0"), sem("scaled_t1")
        turned, xt_hi_made, xt_made = sem("turned"), sem("xt_hi_made"), sem("xt_made")
        slab_read, pool_scaled = sem("slab_read"), sem("pool_scaled")
        up_low, up_summed = sem("up_low"), sem("up_summed")
        up_squared, up_hi, up_made = sem("up_squared"), sem("up_hi"), sem("up_made")
        tail_hi_made, tail_made = sem("tail_hi_made"), sem("tail_made")
        tail_done, c_squared, c_rooted, c_rstd_made = sem("tail_done"), sem("c_squared"), sem("c_rooted"), sem("c_rstd_made")
        c_scaled, c_turned, ct_hi_made, ct_made = sem("c_scaled"), sem("c_turned"), sem("ct_hi_made"), sem("ct_made")
        kr_copied, kr_turned = sem("kr_copied"), sem("kr_turned")
        table_step, angles_made, tables_made = sem("table_step"), sem("angles_made"), sem("tables_made")
        rot_low, rot_step, rot_made, rot_hi, rotated = (sem("rot_low"), sem("rot_step"), sem("rot_made"),
                                                        sem("rot_hi"), sem("rotated"))
        r_summed = sem("r_summed")
        q_low, q_summed, q_hi, q_made = sem("q_low"), sem("q_summed"), sem("q_hi"), sem("q_made")
        k_low, k_summed, k_hi, k_made = sem("k_low"), sem("k_summed"), sem("k_hi"), sem("k_made")
        v_hi_made, v_made = sem("v_hi_made"), sem("v_made")
        scores_done, scores_masked, neg_max_made = sem("scores_done"), sem("scores_masked"), sem("neg_max_made")
        exp_made, inv_made, probs_made = sem("exp_made"), sem("inv_made"), sem("probs_made")
        probs_turned, pt_hi_made, pt_made = sem("probs_turned"), sem("pt_hi_made"), sem("pt_made")
        o_done, o_low, o_summed, o_hi, o_made = (sem("o_done"), sem("o_low"), sem("o_summed"),
                                                 sem("o_hi"), sem("o_made"))
        final_made = sem("final_made")

        block = ctx.enter_context(nc.Block())

        @block.sync
        def _(sp):
            def load(c, source, dyn=0, width=COLS):
                if c >= RAW_SLOTS:
                    sp.wait_ge(lo_made, 2 * (c - RAW_SLOTS) + 2 + dyn)
                sp.dma_start(weight_raw[:, c % RAW_SLOTS, :, 0:width], source).then_inc(raw_in[c % RAW_SLOTS], 16)

            def rows(w, first, n=4):
                return w[first:first + n * P, :].rearrange("(k p) n -> p k n", p=P)

            for t in range(NT):
                sp.dma_start(resid[:, t, :], x[0, t * P:(t + 1) * P, :]).then_inc(x_in[t], 16)
            for slab in range(2):
                for c in range(4):
                    load(U_DQKV // 2 + 4 * slab + c,
                         rows(w_dqkv[0], 4 * P * c)[:, :, slab * COLS:(slab + 1) * COLS])
                    if slab == 0 and c == 0:
                        sp.dma_start(tail_raw, w_dqkv[0, :, 2 * LORA:2 * LORA + ROPE]
                                     .rearrange("(k p) n -> p k n", p=P)).then_inc(tail_in, 16)
            uq = rows(w_uq[0], 0).rearrange("p k (h c) -> p k h c", h=N_HEADS)
            ukv = rows(w_ukv[0], 0).rearrange("p k (h c) -> p k h c", h=N_HEADS)

            def load_heads(c, w, h0, c0, width, dyn, h_dyn):
                if c >= RAW_SLOTS:
                    sp.wait_ge(lo_made, 2 * (c - RAW_SLOTS) + 2 + dyn)
                for k in range(LT):
                    dst = weight_raw[:, c % RAW_SLOTS, k, 0:GH * width].rearrange("p (h c) -> p h c", h=GH)
                    sp.dma_start(dst, w[:, k, bass.ds(h_dyn + h0, GH), c0:c0 + width]).then_inc(
                        raw_in[c % RAW_SLOTS], 16)

            def load_group(c, dyn, h_dyn):
                load_heads(c, uq, 0, 0, NOPE, dyn, h_dyn)
                load_heads(c + 1, ukv, 0, 0, NOPE, dyn, h_dyn)
                load_heads(c + 2, uq, 0, NOPE, ROPE, dyn, h_dyn)
                load_heads(c + 3, ukv, 0, NOPE, V_HEAD, dyn, h_dyn)

            with sp.Fori(0, GROUPS) as g:
                load_group(U_ATT // 2, g * 8, g * GH)
            for slab in range(SLABS):
                for c in range(4):
                    load(U_WO // 2 + 4 * slab + c, rows(w_o[0], 4 * P * c)[:, :, slab * COLS:(slab + 1) * COLS])

            def load_up(layer, c, s, dyn=0):
                for j in range(4):
                    load(c + j, w_up[layer, 4 * P * j:4 * P * (j + 1), bass.ds(s * COLS, COLS)]
                         .rearrange("(k p) n -> p k n", p=P), dyn)

            def load_down(layer, c, s, dyn=0):
                for n in range(SLABS):
                    load(c + n, w_down[layer, bass.ds(s * COLS, COLS), n * COLS:(n + 1) * COLS]
                         .rearrange("(k p) n -> p k n", p=P), dyn)

            def load_mlp(layer):
                c = U_MLP[layer] // 2
                load_up(layer, c, 0)
                with sp.Fori(0, FF_SLABS // 2 - 1) as i:
                    load_up(layer, c + 4, i * 2 + 1, i * 32)
                    load_down(layer, c + 8, i * 2, i * 32)
                    load_up(layer, c + 12, i * 2 + 2, i * 32)
                    load_down(layer, c + 16, i * 2 + 1, i * 32)
                last = c + 4 + 16 * (FF_SLABS // 2 - 1)
                load_up(layer, last, FF_SLABS - 1)
                load_down(layer, last + 4, FF_SLABS - 2)
                load_down(layer, last + 8, FF_SLABS - 1)

            load_mlp(0)
            for g in range(SLABS):
                load(U_POOL // 2 + g, rows(w_pool[0, g], 0))
            load_mlp(1)
            for t in range(NT):
                sp.wait_ge(final_made, t + 1)
                sp.dma_start(out[0, t * P:(t + 1) * P, :], scaled[:, t, :]).then_inc(out_done, 16)
            sp.wait_ge(out_done, 16 * NT)

        @block.gpsimd
        def _(pool):
            pool.dma_start(consts[:, :], shape_consts).then_inc(consts_in, 16)
            for n, (g, rows) in enumerate(((ln_mix, 2 * KT), (ln_mlp, 2 * KT), (q_norm, LT), (kv_norm, LT))):
                first = (0, 2 * KT, 4 * KT, 4 * KT + LT)[n]
                pool.dma_start(gain_rows[first:first + rows, :],
                               g.rearrange("l (k p) -> (l k) p", p=P)).then_inc(gains_in, 16)
            pool.dma_start(pos_i, positions.to_broadcast([P, SEQ])).then_inc(pos_in, 16)
            pool.dma_start(row_gain[:, :], pool_scale.to_broadcast([P, D_MODEL])).then_inc(scale_in, 16)
            pool.wait_ge(probs_turned, GROUPS)
            pool.dma_start(band, band_consts).then_inc(band_in, 16)
            pool.wait_ge(slab_read, S_POOL + SLABS)
            pool.dma_start(row_gain[:, :], final_norm.rearrange("(a n) -> a n", a=1)
                           .to_broadcast([P, D_MODEL])).then_inc(final_in, 16)

        def raw_of(v):
            return weight_raw[:, (v // 2) % RAW_SLOTS, 2 * (v % 2):2 * (v % 2) + 2, :]

        def raw_ready(v):
            c = v // 2
            per = lambda j: 16 * LT if U_ATT // 2 <= j < U_WO // 2 else 16
            return sum(per(j) for j in range(c % RAW_SLOTS, c + 1, RAW_SLOTS))

        def rope_views(dst, v, raw):
            for a in range(2):
                yield (dst[:, v % LEAD, :, a * P:(a + 1) * P].rearrange("p k (h j) -> p k h j", h=GH),
                       raw[:, :, 0:GH * ROPE].rearrange("p k (h a j) -> p k a h j", h=GH, a=2)[:, :, a])

        def is_rope(v):
            return U_ATT <= v < U_WO and (v - U_ATT) % 8 in (4, 5)

        @block.scalar
        def _(act):
            def split(v, dyn=0, raw_dyn=0):
                if v >= U_END:
                    return
                act.wait_ge(raw_in[(v // 2) % RAW_SLOTS], raw_ready(v) + raw_dyn)
                if v >= LEAD:
                    act.wait_ge(unit_used, v - LEAD + 1 + dyn)
                if is_rope(v):
                    for dst, src in rope_views(weight_hi, v, raw_of(v)):
                        last = nc.scalar.copy(dst, src)
                else:
                    last = nc.scalar.copy(weight_hi[:, v % LEAD, :, :], raw_of(v))
                last.then_inc(hi_made, 1)

            def position(k, dyn=0, raw_dyn=0):
                split(k + LEAD, dyn, raw_dyn)

            def square_t0(n):
                nc.scalar.activation(scaled[:, 0, :], resid[:, 0, :], ACT.Square,
                                     accum_out=sumsq[:, 0:1]).then_inc(squared_t0, 1)
                act.wait_ge(squared_t0, n + 1)
                act.wait_ge(squared_t1, n + 1)
                nc.scalar.activation(root, sumsq, ACT.Sqrt, bias=eps, scale=1.0 / D_MODEL).then_inc(rooted, 1)

            def norm(n):
                if n == 0:
                    act.wait_ge(x_in[0], 16)
                    act.wait_ge(eps_set, 1)
                else:
                    act.wait_ge(slab_read, (0, S_MLP[0], S_POOL, S_MLP[1])[n])
                square_t0(n)
                act.wait_ge(rstd_made, n + 1)
                for c in range(4):
                    nc.scalar.activation(scaled[:, 0, c * COLS:(c + 1) * COLS], resid[:, 0, c * COLS:(c + 1) * COLS],
                                         ACT.Copy, scale=rstd[:, 0:1]).then_inc(scaled_t0, 1)
                if n == 0:
                    act.wait_ge(gains_turned, 1)
                    nc.scalar.copy(gain_col[:, :], ps[:, 7, 0:N_GAINS]).then_inc(gains_ready, 1)
                    act.wait_ge(gains_ready, 1)
                for k in range(KT):
                    act.wait_ge(turned, 8 * n + k // 2 + 1)
                    nc.scalar.activation(xt[:, k, 0:SEQ], ps[:, k // 2, (k % 2) * SEQ:(k % 2 + 1) * SEQ], ACT.Copy,
                                         scale=gain_col[:, GAIN_COL[n] + k:GAIN_COL[n] + k + 1]).then_inc(xt_hi_made, 1)

            def c_norm(j):
                act.wait_ge(unit_used, U_DQKV + 8 * (j + 1))
                for t in range(NT):
                    nc.scalar.activation(latent[:, t, j * LORA:(j + 1) * LORA], ps[:, 4 + 2 * j + t, :], ACT.Square,
                                         accum_out=c_sumsq[:, j, t:t + 1]).then_inc(c_squared, 1)
                act.wait_ge(c_squared, 2 * j + 2)
                nc.scalar.activation(c_root[:, j, :], c_sumsq[:, j, :], ACT.Sqrt, bias=eps,
                                     scale=1.0 / LORA).then_inc(c_rooted, 1)
                act.wait_ge(c_rstd_made, j + 1)
                for t in range(NT):
                    nc.scalar.activation(latent[:, t, j * LORA:(j + 1) * LORA], ps[:, 4 + 2 * j + t, :], ACT.Copy,
                                         scale=c_rstd[:, j, t:t + 1]).then_inc(c_scaled, 1)
                for k in range(LT):
                    act.wait_ge(c_turned, 2 * j + k // 2 + 1)
                    g = Q_GAIN + j * LT + k
                    nc.scalar.activation(latent_t[:, j * LT + k, 0:SEQ],
                                         ps[:, 2 * j + k // 2, (k % 2) * SEQ:(k % 2 + 1) * SEQ], ACT.Copy,
                                         scale=gain_col[:, g:g + 1]).then_inc(ct_hi_made, 1)

            def fold_low(k, dyn, low, side):
                act.wait_ge(unit_used, k + 1 + dyn)
                nc.scalar.copy(fold_b[side], ps[:, 4 * side:4 * side + 4, SEQ:2 * SEQ]).then_inc(low, 1)

            def round_hi(n, dyn, value_made, dst, value, hi):
                act.wait_ge(value_made, n + 1 + dyn)
                nc.scalar.copy(dst, value).then_inc(hi, 1)

            norm(0)
            for v in range(LEAD):
                split(v)
            for k in range(U_DQKV, U_ATT):
                position(k)
                if k == 2:
                    act.wait_ge(tail_in, 16)
                    nc.scalar.copy(tail_hi, tail_raw).then_inc(tail_hi_made, 1)
                if k == 4:
                    act.wait_ge(angles_made, 1)
                    for a in range(2):
                        nc.scalar.activation(sin_t[:, a, :], rot_c[:, 0, :], ACT.Sin).then_inc(tables_made, 1)
                        nc.scalar.activation(cos_t[:, a, :], rot_c[:, 1, :], ACT.Sin).then_inc(tables_made, 1)
                if k == 7:
                    c_norm(0)
            c_norm(1)
            act.wait_ge(tail_done, 1)
            for r in range(4):
                last = nc.scalar.copy(k_rope[:, :, :, r, :],
                                      ps[:, 4:6, 0:ROPE].rearrange("p t (a j) -> p t a j", a=2))
            last.then_inc(kr_copied, 1)
            round_hi(0, 0, rot_made, kr_t[:, :, 0:SEQ], rot_x, rot_hi)

            def q_fold(g, dyn=0):
                fold_low(U_ATT + 8 * g + 1, dyn * 8, q_low, 0)
                round_hi(g, dyn, q_summed, q_t[:, :, 0:SEQ], fold_s[0], q_hi)

            def k_fold(g, dyn=0):
                fold_low(U_ATT + 8 * g + 3, dyn * 8, k_low, 1)
                round_hi(g, dyn, k_summed, k_t[:, :, 0:SEQ], fold_s[1], k_hi)

            def r_fold(g, dyn=0):
                act.wait_ge(unit_used, U_ATT + 8 * g + 6 + dyn * 8)
                nc.scalar.copy(rot_b, ps[:, 4:6, SEQ:2 * SEQ]).then_inc(rot_low, 1)
                round_hi(g + 1, dyn, rot_made, qr_t[:, :, 0:SEQ], rot_x, rot_hi)

            def v_round(g, dyn=0):
                act.wait_ge(unit_used, U_ATT + 8 * g + 8 + dyn * 8)
                nc.scalar.copy(v_hi[:, :, :], ps[:, 6:8, :]).then_inc(v_hi_made, 1)

            def exps(g, dyn=0):
                act.wait_ge(neg_max_made, g + 1 + dyn)
                for h in range(GH):
                    for t in range(NT):
                        i = NT * h + t
                        part = probs[:, h, SCORE_COLS[t][0]:SCORE_COLS[t][1]]
                        nc.scalar.activation(part, part, ACT.Exp, bias=neg_max[:, i:i + 1], scale=SCALE,
                                             accum_out=row_sum[:, i:i + 1]).then_inc(exp_made, 1)

            def pt_round(g, dyn=0):
                act.wait_ge(probs_turned, g + 1 + dyn)
                nc.scalar.copy(p_t[:, :, 0:2 * P], ps[:, 0:4, 0:2 * P]).then_inc(pt_hi_made, 1)
                nc.scalar.copy(p_t[:, :, 4 * P:5 * P], ps[:, 0:4, 2 * P:3 * P]).then_inc(pt_hi_made, 1)

            def o_fold(g, dyn=0):
                act.wait_ge(o_done, g + 1 + dyn)
                nc.scalar.copy(fold_b[0], ps[:, 0:4, SEQ:2 * SEQ]).then_inc(o_low, 1)
                act.wait_ge(o_summed, g + 1 + dyn)
                nc.scalar.copy(xt[:, bass.ds(dyn * GH + g * GH, GH), 0:SEQ], fold_s[0]).then_inc(o_hi, 1)

            def attention_step(g, i=0):
                b, dyn, raw_dyn = U_ATT + 8 * (g + 1), i * 8, i * 16 * LT
                exps(g, i)
                position(b, dyn, raw_dyn)
                position(b + 1, dyn, raw_dyn)
                q_fold(g + 1, i)
                position(b + 2, dyn, raw_dyn)
                position(b + 3, dyn, raw_dyn)
                k_fold(g + 1, i)
                pt_round(g, i)
                position(b + 4, dyn, raw_dyn)
                position(b + 5, dyn, raw_dyn)
                r_fold(g + 1, i)
                o_fold(g, i)
                position(b + 6, dyn, raw_dyn)
                position(b + 7, dyn, raw_dyn)
                v_round(g + 1, i)

            for k in range(U_ATT, U_ATT + 8):
                position(k)
                if k == U_ATT + 1:
                    q_fold(0)
                if k == U_ATT + 3:
                    k_fold(0)
                if k == U_ATT + 5:
                    r_fold(0)
            v_round(0)
            with act.Fori(0, GROUPS - 2) as i:
                attention_step(0, i)
            attention_step(GROUPS - 2)
            exps(GROUPS - 1)
            pt_round(GROUPS - 1)
            o_fold(GROUPS - 1)

            with act.Fori(0, SLABS // 2) as i:
                for k in range(16):
                    position(U_WO + k, i * 16, i * 32)

            def mlp(layer):
                s0 = layer * FF_SLABS

                def up(b, s, dyn=0, raw_dyn=0, s_dyn=0):
                    for k in range(8):
                        position(b + k, dyn, raw_dyn)
                    fold_low(b + 7, dyn, up_low, 0)

                def square_hi(s, s_dyn=0):
                    round_hi(s0 + s, s_dyn, up_squared, mid[:, s % 2, :, 0:SEQ], fold_s[1], up_hi)

                def down(b, s_up, dyn=0, raw_dyn=0, s_dyn=0):
                    for k in range(8):
                        position(b + k, dyn, raw_dyn)
                        if s_up is not None and k == 1:
                            square_hi(s_up, s_dyn)

                b = U_MLP[layer]
                up(b, 0)
                square_hi(0)
                with act.Fori(0, FF_SLABS // 2 - 1) as i:
                    up(b + 8, 1, i * 32, i * 64, i * 2)
                    down(b + 16, 1, i * 32, i * 64, i * 2)
                    up(b + 24, 2, i * 32, i * 64, i * 2)
                    down(b + 32, 2, i * 32, i * 64, i * 2)
                b = U_MLP[layer] + 16 * FF_SLABS - 24
                up(b, FF_SLABS - 1)
                down(b + 8, FF_SLABS - 1)
                down(b + 16, None)

            norm(1)
            mlp(0)
            norm(2)
            for k in range(U_POOL, U_MLP[1]):
                position(k)
            norm(3)
            mlp(1)
            act.wait_ge(slab_read, S_END)
            square_t0(4)

        @block.vector
        def _(dve):
            def as_f32(a):
                return a.bitcast(F32)

            def split(v, dyn=0):
                if v >= U_END:
                    return
                dve.wait_ge(hi_made, v + 1 + dyn)
                if is_rope(v):
                    for (dst, src), (hi, _) in zip(rope_views(weight_lo, v, raw_of(v)),
                                                   rope_views(weight_hi, v, raw_of(v))):
                        last = nc.vector.tensor_tensor(dst, src, as_f32(hi), ALU.subtract)
                else:
                    last = nc.vector.tensor_tensor(weight_lo[:, v % LEAD, :, :], raw_of(v),
                                                   as_f32(weight_hi[:, v % LEAD, :, :]), ALU.subtract)
                last.then_inc(lo_made, 1)

            def position(k, dyn=0):
                split(k + LEAD, dyn)

            def square_t1(n):
                nc.vector.tensor_tensor_reduce(out=scaled[:, 1, :], in0=resid[:, 1, :], in1=resid[:, 1, :],
                                               scale=1.0, scalar=0.0, op0=ALU.mult, op1=ALU.add,
                                               accum_out=sumsq[:, 1:2]).then_inc(squared_t1, 1)
                dve.wait_ge(rooted, n + 1)
                nc.vector.reciprocal(rstd, root).then_inc(rstd_made, 1)
                dve.wait_ge(rstd_made, n + 1)

            def norm(n):
                if n == 0:
                    nc.vector.memset(eps, EPS).then_inc(eps_set, 1)
                    dve.wait_ge(x_in[1], 16)
                else:
                    dve.wait_ge(slab_read, (0, S_MLP[0], S_POOL, S_MLP[1])[n])
                square_t1(n)
                for c in range(4):
                    nc.vector.tensor_scalar(scaled[:, 1, c * COLS:(c + 1) * COLS], resid[:, 1, c * COLS:(c + 1) * COLS],
                                            rstd[:, 1:2], None, ALU.mult).then_inc(scaled_t1, 1)
                for k in range(KT):
                    dve.wait_ge(xt_hi_made, KT * n + k // 2 * 2 + 2)
                    g = GAIN_COL[n] + k
                    nc.vector.scalar_tensor_tensor(
                        out=xt[:, k, SEQ:2 * SEQ], in0=ps[:, k // 2, (k % 2) * SEQ:(k % 2 + 1) * SEQ],
                        scalar=gain_col[:, g:g + 1], in1=as_f32(xt[:, k, 0:SEQ]),
                        op0=ALU.mult, op1=ALU.subtract).then_inc(xt_made, 1)

            def c_norm(j):
                dve.wait_ge(c_rooted, j + 1)
                nc.vector.reciprocal(c_rstd[:, j, :], c_root[:, j, :]).then_inc(c_rstd_made, 1)
                for k in range(LT):
                    dve.wait_ge(ct_hi_made, LT * j + k // 2 * 2 + 2)
                    g = Q_GAIN + j * LT + k
                    nc.vector.scalar_tensor_tensor(
                        out=latent_t[:, j * LT + k, SEQ:2 * SEQ],
                        in0=ps[:, 2 * j + k // 2, (k % 2) * SEQ:(k % 2 + 1) * SEQ],
                        scalar=gain_col[:, g:g + 1], in1=as_f32(latent_t[:, j * LT + k, 0:SEQ]),
                        op0=ALU.mult, op1=ALU.subtract).then_inc(ct_made, 1)

            def rope_angles():
                steps = [0]

                def then_wait(instruction):
                    steps[0] += 1
                    instruction.then_inc(table_step, 1)
                    dve.wait_ge(table_step, steps[0])

                angle, turns, r = rot_s[:, 0, :], rot_s[:, 1, :], rot_c[:, 0, :]
                shifted, wrap = rot_c[:, 1, :], rot_s[:, 0, :]
                dve.wait_ge(pos_in, 16)
                dve.wait_ge(consts_in, 16)
                dve.wait_ge(turned, 8)
                then_wait(nc.vector.tensor_copy(turns, pos_i))
                then_wait(nc.vector.tensor_scalar(angle, turns, inv_freq, None, ALU.mult))
                then_wait(nc.vector.tensor_scalar(turns, angle, 0.5 / math.pi, ROUNDER, ALU.mult, ALU.add))
                then_wait(nc.vector.tensor_scalar(turns, turns, ROUNDER, None, ALU.subtract))
                then_wait(nc.vector.scalar_tensor_tensor(out=r, in0=turns, scalar=-TWO_PI_A, in1=angle,
                                                         op0=ALU.mult, op1=ALU.add))
                for part in (TWO_PI_B, TWO_PI_C):
                    then_wait(nc.vector.scalar_tensor_tensor(out=r, in0=turns, scalar=-part, in1=r,
                                                             op0=ALU.mult, op1=ALU.add))
                then_wait(nc.vector.tensor_scalar(shifted, r, 0.5 * math.pi, None, ALU.add))
                then_wait(nc.vector.tensor_scalar(wrap, shifted, math.pi, -2.0 * math.pi, ALU.is_gt, ALU.mult))
                then_wait(nc.vector.tensor_tensor(shifted, shifted, wrap, ALU.add))
                nc.vector.tensor_scalar(rot_c, rot_c, PI_IN, -PI_IN, ALU.min, ALU.max).then_inc(angles_made, 1)

            def rotate(n, source, dst, dyn=0):
                nc.vector.tensor_tensor(rot_c, source, cos_t[:, :, :], ALU.mult).then_inc(rot_step, 1)
                nc.vector.tensor_tensor(rot_s, source, sin_t[:, :, :], ALU.mult).then_inc(rot_step, 1)
                dve.wait_ge(rot_step, 2 * n + 2 + 2 * dyn)
                nc.vector.tensor_tensor(rot_x[:, 0, :], rot_c[:, 0, :], rot_s[:, 1, :], ALU.subtract)
                nc.vector.tensor_tensor(rot_x[:, 1, :], rot_c[:, 1, :], rot_s[:, 0, :],
                                        ALU.add).then_inc(rot_made, 1)
                dve.wait_ge(rot_hi, n + 1 + dyn)
                nc.vector.tensor_tensor(dst[:, :, SEQ:2 * SEQ], rot_x, as_f32(dst[:, :, 0:SEQ]),
                                        ALU.subtract).then_inc(rotated, 1)

            def fold_sum(n, dyn, low, summed, side):
                dve.wait_ge(low, n + 1 + dyn)
                nc.vector.tensor_tensor(fold_s[side], ps[:, 4 * side:4 * side + 4, 0:SEQ], fold_b[side],
                                        ALU.add).then_inc(summed, 1)

            def subtract_hi(n, dyn, value, dst, hi, made):
                dve.wait_ge(hi, n + 1 + dyn)
                nc.vector.tensor_tensor(dst[:, :, SEQ:2 * SEQ], value, as_f32(dst[:, :, 0:SEQ]),
                                        ALU.subtract).then_inc(made, 1)

            def q_fold(g, dyn=0):
                fold_sum(g, dyn, q_low, q_summed, 0)
                subtract_hi(g, dyn, fold_s[0], q_t, q_hi, q_made)

            def k_fold(g, dyn=0):
                fold_sum(g, dyn, k_low, k_summed, 1)
                subtract_hi(g, dyn, fold_s[1], k_t, k_hi, k_made)

            def r_fold(g, dyn=0):
                dve.wait_ge(rot_low, g + 1 + dyn)
                nc.vector.tensor_tensor(rot_x, ps[:, 4:6, 0:SEQ], rot_b, ALU.add).then_inc(r_summed, 1)
                dve.wait_ge(r_summed, g + 1 + dyn)
                rotate(g + 1, rot_x, qr_t, dyn)

            def v_low(g, dyn=0):
                dve.wait_ge(v_hi_made, g + 1 + dyn)
                nc.vector.tensor_tensor(v_lo[:, :, :], ps[:, 6:8, :], as_f32(v_hi[:, :, :]),
                                        ALU.subtract).then_inc(v_made, 1)

            def mask_scores(g, dyn=0):
                for h in range(GH):
                    if h % 2 == 0:
                        dve.wait_ge(scores_done, 2 * g + h // 2 + 1 + dyn * 2)
                        nc.vector.memset(step_mark[:, h // 2:h // 2 + 1], 0.0)
                    for t in range(NT):
                        lo, hi = SCORE_COLS[t]
                        i = NT * h + t
                        nc.vector.tensor_tensor_reduce(
                            out=probs[:, h, lo:hi], in0=ps[:, 4 + h, lo:hi], in1=causal[:, (1 - t) * P:2 * P],
                            scale=1.0, scalar=-3.4e38, op0=ALU.add, op1=ALU.max,
                            accum_out=row_max[:, i:i + 1]).then_inc(scores_masked, 1)
                dve.wait_ge(scores_masked, 8 * (g + 1) + dyn * 8)
                nc.vector.tensor_scalar(neg_max, row_max, -SCALE, None, ALU.mult).then_inc(neg_max_made, 1)

            def normalise(g, dyn=0):
                dve.wait_ge(exp_made, 8 * (g + 1) + dyn * 8)
                nc.vector.reciprocal(inv_sum, row_sum).then_inc(inv_made, 1)
                dve.wait_ge(inv_made, g + 1 + dyn)
                for h in range(GH):
                    for t in range(NT):
                        i = NT * h + t
                        part = probs[:, h, SCORE_COLS[t][0]:SCORE_COLS[t][1]]
                        nc.vector.tensor_scalar(part, part, inv_sum[:, i:i + 1], None, ALU.mult).then_inc(probs_made, 1)

            def pt_low(g, dyn=0):
                dve.wait_ge(pt_hi_made, 2 * (g + 1) + dyn * 2)
                nc.vector.tensor_tensor(p_t[:, :, 2 * P:4 * P], ps[:, 0:4, 0:2 * P], as_f32(p_t[:, :, 0:2 * P]),
                                        ALU.subtract).then_inc(pt_made, 1)
                nc.vector.tensor_tensor(p_t[:, :, 5 * P:6 * P], ps[:, 0:4, 2 * P:3 * P],
                                        as_f32(p_t[:, :, 4 * P:5 * P]), ALU.subtract).then_inc(pt_made, 1)

            def o_fold(g, dyn=0):
                fold_sum(g, dyn, o_low, o_summed, 0)
                dve.wait_ge(o_hi, g + 1 + dyn)
                heads = xt[:, bass.ds(dyn * GH + g * GH, GH), :]
                nc.vector.tensor_tensor(heads[:, :, SEQ:2 * SEQ], fold_s[0], as_f32(heads[:, :, 0:SEQ]),
                                        ALU.subtract).then_inc(o_made, 1)

            def attention_step(g, i=0):
                b, dyn = U_ATT + 8 * (g + 1), i * 8
                mask_scores(g, i)
                position(b, dyn)
                position(b + 1, dyn)
                q_fold(g + 1, i)
                normalise(g, i)
                position(b + 2, dyn)
                position(b + 3, dyn)
                k_fold(g + 1, i)
                pt_low(g, i)
                position(b + 4, dyn)
                position(b + 5, dyn)
                r_fold(g + 1, i)
                o_fold(g, i)
                position(b + 6, dyn)
                position(b + 7, dyn)
                v_low(g + 1, i)

            def add_slab(k, s, n, dyn=0, s_dyn=0):
                dve.wait_ge(unit_used, k + 1 + dyn)
                if s >= 1:
                    dve.wait_ge(slab_read, s + s_dyn)
                for t in range(NT):
                    cols = resid[:, t, n * COLS:(n + 1) * COLS]
                    last = nc.vector.tensor_tensor(cols, ps[:, 4 + 2 * (n % 2) + t, :], cols, ALU.add)
                last.then_inc(slab_read, 1)

            norm(0)
            for v in range(LEAD):
                split(v)
            for k in range(U_DQKV, U_ATT):
                position(k)
                if k == 1:
                    rope_angles()
                if k == 3:
                    dve.wait_ge(tail_hi_made, 1)
                    nc.vector.tensor_tensor(tail_lo, tail_raw, as_f32(tail_hi), ALU.subtract).then_inc(tail_made, 1)
                if k == 7:
                    c_norm(0)
            c_norm(1)
            dve.wait_ge(kr_turned, 1)
            dve.wait_ge(tables_made, 4)
            rotate(0, ps[:, 6, :].rearrange("p (a n) -> p a n", a=2), kr_t)
            for k in range(U_ATT, U_ATT + 8):
                position(k)
                if k == U_ATT + 1:
                    q_fold(0)
                if k == U_ATT + 3:
                    k_fold(0)
                if k == U_ATT + 5:
                    r_fold(0)
            v_low(0)
            with dve.Fori(0, GROUPS - 2) as i:
                attention_step(0, i)
            attention_step(GROUPS - 2)
            mask_scores(GROUPS - 1)
            normalise(GROUPS - 1)
            pt_low(GROUPS - 1)
            o_fold(GROUPS - 1)

            for n in range(SLABS):
                for k in range(8):
                    position(U_WO + 8 * n + k)
                add_slab(U_WO + 8 * n + 7, S_WO + n, n)

            def mlp(layer):
                s0 = layer * FF_SLABS

                def up(b, s, dyn=0, s_dyn=0):
                    for k in range(8):
                        position(b + k, dyn)
                    fold_sum(s0 + s, s_dyn, up_low, up_summed, 0)

                def square(s, s_dyn=0):
                    dve.wait_ge(up_summed, s0 + s + 1 + s_dyn)
                    nc.vector.scalar_tensor_tensor(out=fold_s[1], in0=fold_s[0], scalar=0.0, in1=fold_s[0],
                                                   op0=ALU.max, op1=ALU.mult).then_inc(up_squared, 1)

                def square_low(s, s_dyn=0):
                    subtract_hi(s0 + s, s_dyn, fold_s[1], mid[:, s % 2, :, :], up_hi, up_made)

                def down(b, s, s_up, dyn=0, s_dyn=0):
                    for k in range(8):
                        position(b + k, dyn)
                        if s_up is not None and k == 0:
                            square(s_up, s_dyn)
                        if s_up is not None and k == 2:
                            square_low(s_up, s_dyn)
                        if k % 2 == 1:
                            add_slab(b + k, S_MLP[layer] + s * SLABS + k // 2, k // 2, dyn, s_dyn * SLABS)

                b = U_MLP[layer]
                up(b, 0)
                square(0)
                square_low(0)
                with dve.Fori(0, FF_SLABS // 2 - 1) as i:
                    up(b + 8, 1, i * 32, i * 2)
                    down(b + 16, 0, 1, i * 32, i * 2)
                    up(b + 24, 2, i * 32, i * 2)
                    down(b + 32, 1, 2, i * 32, i * 2)
                b = U_MLP[layer] + 16 * FF_SLABS - 24
                up(b, FF_SLABS - 1)
                down(b + 8, FF_SLABS - 2, FF_SLABS - 1)
                down(b + 16, FF_SLABS - 1, None)

            norm(1)
            mlp(0)
            norm(2)
            dve.wait_ge(scale_in, 16)
            for g in range(SLABS):
                position(U_POOL + 2 * g)
                position(U_POOL + 2 * g + 1)
                dve.wait_ge(unit_used, U_POOL + 2 * g + 2)
                for t in range(NT):
                    nc.vector.tensor_tensor(scaled[:, t, g * COLS:(g + 1) * COLS], ps[:, 4 + 2 * (g % 2) + t, :],
                                            row_gain[:, g * COLS:(g + 1) * COLS], ALU.mult).then_inc(pool_scaled, 1)
                dve.wait_ge(pool_scaled, NT * (g + 1))
                for t in range(NT):
                    cols = resid[:, t, g * COLS:(g + 1) * COLS]
                    last = nc.vector.tensor_tensor(cols, scaled[:, t, g * COLS:(g + 1) * COLS], cols, ALU.add)
                last.then_inc(slab_read, 1)
            norm(3)
            mlp(1)
            dve.wait_ge(slab_read, S_END)
            square_t1(4)
            dve.wait_ge(final_in, 16)
            for t in range(NT):
                nc.vector.scalar_tensor_tensor(out=scaled[:, t, :], in0=resid[:, t, :], scalar=rstd[:, t:t + 1],
                                               in1=row_gain[:, :], op0=ALU.mult, op1=ALU.mult).then_inc(final_made, 1)

        @block.tensor
        def _(pe):
            mm = nc.tensor.matmul

            def token_unit(k, source, tile, bank, first, last, dyn=0):
                pe.wait_ge(lo_made, k + 1 + dyn)
                s = k % LEAD
                for j in range(2):
                    for t in range(NT):
                        hi = source[:, tile + j, t * P:(t + 1) * P]
                        lo = source[:, tile + j, SEQ + t * P:SEQ + (t + 1) * P]
                        o = ps[:, bank + t, :]
                        mm(o, hi, weight_hi[:, s, j, :], start=first and j == 0, stop=False)
                        mm(o, hi, weight_lo[:, s, j, :], start=False, stop=False)
                        end = mm(o, lo, weight_hi[:, s, j, :], start=False, stop=last and j == 1)
                end.then_inc(unit_used, 1)

            def weight_unit(k, source, tile, bank, first, last, dyn=0, blocks=FB):
                pe.wait_ge(lo_made, k + 1 + dyn)
                s = k % LEAD
                for j in range(2):
                    for f in range(blocks):
                        w_hi = weight_hi[:, s, j, f * P:(f + 1) * P]
                        w_lo = weight_lo[:, s, j, f * P:(f + 1) * P]
                        both = (w_hi, source[:, tile + j, :], ps[:, bank + f, :])
                        high = (w_lo, source[:, tile + j, 0:SEQ], ps[:, bank + f, 0:SEQ])
                        order = (high, both) if j == 1 else (both, high)
                        for i, (w, m, o) in enumerate(order):
                            end = mm(o, w, m, start=first and j == 0 and i == 0, stop=last and j == 1 and i == 1)
                end.then_inc(unit_used, 1)

            def norm(n):
                for b in range(8):
                    if b % 2 == 0:
                        pe.wait_ge(scaled_t0, 4 * n + b // 2 + 1)
                        pe.wait_ge(scaled_t1, 4 * n + b // 2 + 1)
                    if n == 0 and b == 7:
                        pe.wait_ge(gains_ready, 1)
                    for a in range(2):
                        cols = slice((2 * b + a) * P, (2 * b + a + 1) * P)
                        if n == 2:
                            g = (2 * b + a) // LT
                            mm(ps[:, b, a * SEQ:(a + 1) * SEQ], scaled[:, 0, cols],
                               band[:, g * SEQ:(g + 1) * SEQ], start=True, stop=False)
                            end = mm(ps[:, b, a * SEQ + P:(a + 1) * SEQ], scaled[:, 1, cols],
                                     band[:, 4 * SEQ + g * P:4 * SEQ + (g + 1) * P], start=False, stop=True)
                        else:
                            for t in range(NT):
                                end = nc.tensor.transpose(ps[:, b, a * SEQ + t * P:a * SEQ + (t + 1) * P],
                                                          scaled[:, t, cols], ident)
                    end.then_inc(turned, 1)

            def xt_ready(n, k):
                pe.wait_ge(xt_made, KT * n + k + 1)

            def c_turn(j):
                pe.wait_ge(c_scaled, NT * (j + 1))
                for b in range(2):
                    for a in range(2):
                        for t in range(NT):
                            f = j * LORA + (2 * b + a) * P
                            end = nc.tensor.transpose(ps[:, 2 * j + b, a * SEQ + t * P:a * SEQ + (t + 1) * P],
                                                      latent[:, t, f:f + P], ident)
                    end.then_inc(c_turned, 1)

            pe.wait_ge(consts_in, 16)
            pe.wait_ge(gains_in, 64)
            nc.tensor.transpose(ps[:, 7, 0:N_GAINS], gain_rows, ident[0:N_GAINS, 0:N_GAINS]).then_inc(gains_turned, 1)
            norm(0)
            for slab in range(2):
                for u in range(8):
                    if slab == 0:
                        xt_ready(0, 2 * u + 1)
                    token_unit(U_DQKV + 8 * slab + u, xt, 2 * u, 4 + 2 * slab, u == 0, u == 7)
                    if slab == 1 and u == 1:
                        pe.wait_ge(xt_made, KT)
                        c_turn(0)
            pe.wait_ge(tail_made, 1)
            for t in range(NT):
                for k in range(KT):
                    hi, lo = xt[:, k, t * P:(t + 1) * P], xt[:, k, SEQ + t * P:SEQ + (t + 1) * P]
                    o = ps[:, 4 + t, 0:ROPE]
                    mm(o, hi, tail_hi[:, k, :], start=k == 0, stop=False)
                    mm(o, hi, tail_lo[:, k, :], start=False, stop=False)
                    end = mm(o, lo, tail_hi[:, k, :], start=False, stop=k == KT - 1)
            end.then_inc(tail_done, 1)
            c_turn(1)
            pe.wait_ge(kr_copied, 1)
            for a in range(2):
                for t in range(NT):
                    end = nc.tensor.transpose(ps[:, 6, a * SEQ + t * P:a * SEQ + (t + 1) * P],
                                              k_rope[:, t, a, :, :].rearrange("p r j -> p (r j)"), ident)
            end.then_inc(kr_turned, 1)

            def project_q(g, i=0):
                b = U_ATT + 8 * g
                for u in range(2):
                    weight_unit(b + u, latent_t, 2 * u, 0, u == 0, u == 1, i * 8)

            def project_k(g, i=0):
                b = U_ATT + 8 * g + 2
                for u in range(2):
                    weight_unit(b + u, latent_t, LT + 2 * u, 4, u == 0, u == 1, i * 8)

            def project_rope(g, i=0):
                pe.wait_ge(k_summed, g + 1 + i)
                b = U_ATT + 8 * g + 4
                for u in range(2):
                    weight_unit(b + u, latent_t, 2 * u, 4, u == 0, u == 1, i * 8, blocks=2)

            def project_v(g, i=0):
                b = U_ATT + 8 * g + 6
                for u in range(2):
                    token_unit(b + u, latent_t, LT + 2 * u, 6, u == 0, u == 1, i * 8)

            def scores(g, i=0):
                pe.wait_ge(q_made, g + 1 + i)
                pe.wait_ge(k_made, g + 1 + i)
                pe.wait_ge(rotated, g + 2 + i)
                for h in range(GH):
                    if h == 2:
                        pe.wait_ge(v_made, g + 1 + i)
                    for t in range(NT):
                        lo, hi = SCORE_COLS[t]
                        o, keys = ps[:, 4 + h, lo:hi], (t + 1) * P

                        def three(rows, q, k, start, stop):
                            q_hi, q_lo = q[rows, t * P:(t + 1) * P], q[rows, SEQ + t * P:SEQ + (t + 1) * P]
                            k_hi, k_lo = k[rows, 0:keys], k[rows, SEQ:SEQ + keys]
                            mm(o, q_hi, k_hi, start=start, stop=False)
                            mm(o, q_hi, k_lo, start=False, stop=False)
                            return mm(o, q_lo, k_hi, start=False, stop=stop)

                        three(slice(0, P), q_t[:, h, :], k_t[:, h, :], True, False)
                        rows = slice(h * HALF, (h + 1) * HALF)
                        three(rows, qr_t[:, 0, :], kr_t[:, 0, :], False, False)
                        end = three(rows, qr_t[:, 1, :], kr_t[:, 1, :], False, True)
                    if h % 2 == 1:
                        end.then_inc(scores_done, 1)

            def turn_probs(g, i=0):
                pe.wait_ge(probs_made, 8 * (g + 1) + i * 8)
                pe.wait_ge(q_summed, min(g + 2, GROUPS) + i)
                for h in range(GH):
                    for c in (0, P, 2 * P):
                        end = nc.tensor.transpose(ps[:, h, c:c + P], probs[:, h, c:c + P], ident)
                end.then_inc(probs_turned, 1)

            def values(g, i=0):
                pe.wait_ge(pt_made, 2 * (g + 1) + i * 2)
                pe.wait_ge(v_made, g + 1 + i)
                for h in range(GH):
                    c = slice(h * V_HEAD, (h + 1) * V_HEAD)
                    halves = ps[:, h, :].rearrange("p (a n) -> p a n", a=2)
                    mm(ps[:, h, :], v_hi[:, 0, c], p_t[:, h, 0:4 * P], start=True, stop=False)
                    mm(ps[:, h, 0:SEQ], v_lo[:, 0, c], p_t[:, h, 0:2 * P], start=False, stop=False)
                    mm(ps[:, h, P:SEQ], v_lo[:, 1, c], p_t[:, h, 4 * P:5 * P], start=False, stop=False)
                    end = mm(halves[:, :, P:2 * P], v_hi[:, 1, c],
                             p_t[:, h, 4 * P:6 * P].rearrange("p (a n) -> p a n", a=2), start=False, stop=True)
                end.then_inc(o_done, 1)

            def attention_step(g, i=0):
                scores(g, i)
                if g > 0:
                    pe.wait_ge(o_summed, g + i)
                project_q(g + 1, i)
                pe.wait_ge(scores_masked, 8 * (g + 1) + i * 8)
                project_k(g + 1, i)
                turn_probs(g, i)
                project_rope(g + 1, i)
                values(g, i)
                project_v(g + 1, i)

            pe.wait_ge(ct_made, 2 * LT)
            project_q(0)
            pe.wait_ge(rot_step, 2)
            project_k(0)
            project_rope(0)
            project_v(0)
            attention_step(0)
            with pe.Fori(0, GROUPS - 2) as i:
                attention_step(1, i)
            scores(GROUPS - 1)
            turn_probs(GROUPS - 1)
            values(GROUPS - 1)

            pe.wait_ge(o_made, GROUPS)
            for n in range(SLABS):
                if n >= 2:
                    pe.wait_ge(slab_read, S_WO + n - 1)
                for u in range(8):
                    token_unit(U_WO + 8 * n + u, xt, 2 * u, 4 + 2 * (n % 2), u == 0, u == 7)

            def mlp(layer, norm_index):
                s0 = layer * FF_SLABS

                def up(b, s, dyn=0, s_dyn=0):
                    if s0 + s >= 1:
                        pe.wait_ge(up_summed, s0 + s + s_dyn)
                    for u in range(8):
                        if s == 0:
                            xt_ready(norm_index, max(2 * u + 1, 7))
                        weight_unit(b + u, xt, 2 * u, 0, u == 0, u == 7, dyn)

                def down(b, s, dyn=0, s_dyn=0):
                    pe.wait_ge(up_made, s0 + s + 1 + s_dyn)
                    for n in range(SLABS):
                        pe.wait_ge(slab_read, S_MLP[layer] + s * SLABS + n - 1 + s_dyn * SLABS)
                        for u in range(2):
                            token_unit(b + 2 * n + u, mid[:, s % 2, :, :], 2 * u, 4 + 2 * (n % 2),
                                       u == 0, u == 1, dyn)

                b = U_MLP[layer]
                up(b, 0)
                with pe.Fori(0, FF_SLABS // 2 - 1) as i:
                    up(b + 8, 1, i * 32, i * 2)
                    down(b + 16, 0, i * 32, i * 2)
                    up(b + 24, 2, i * 32, i * 2)
                    down(b + 32, 1, i * 32, i * 2)
                b = U_MLP[layer] + 16 * FF_SLABS - 24
                up(b, FF_SLABS - 1)
                down(b + 8, FF_SLABS - 2)
                down(b + 16, FF_SLABS - 1)

            norm(1)
            mlp(0, 1)
            pe.wait_ge(band_in, 16)
            norm(2)
            for g in range(SLABS):
                xt_ready(2, LT * g + LT - 1)
                if g == 0:
                    xt_ready(2, KT - 1)
                if g >= 2:
                    pe.wait_ge(slab_read, S_POOL + g - 1)
                for u in range(2):
                    token_unit(U_POOL + 2 * g + u, xt, LT * g + 2 * u, 4 + 2 * (g % 2), u == 0, u == 1)
            norm(3)
            mlp(1, 3)


_INS = ["x", "positions", "ln_mix", "ln_mlp", "w_dqkv", "q_norm", "kv_norm", "w_uq", "w_ukv", "w_o",
        "w_pool", "pool_scale", "w_up", "w_down", "final_norm"]


def shape_constants():
    causal = np.zeros((P, 2 * P), np.float32)
    causal[:, P:] = np.where(np.arange(P)[None, :] <= np.arange(P)[:, None], 0.0, MASKED)
    exponent = np.arange(0, ROPE, 2, dtype=np.float32) / np.float32(ROPE)
    inv_freq = (np.float32(1.0) / np.power(np.float32(ROPE_THETA), exponent)).astype(np.float32)
    first = np.concatenate([np.eye(P, dtype=np.float32), causal, np.tile(inv_freq, P // HALF)[:, None]], axis=1)
    s, t = np.arange(SEQ)[:, None], np.arange(SEQ)[None, :]
    bands = []
    for w in WINDOWS:
        inside = (s <= t) & (s > t - w)
        bands.append((inside / np.minimum(t + 1, w) - (s == t)).astype(np.float32))
    second = np.concatenate([b[0:P, :] for b in bands] + [b[P:, P:] for b in bands], axis=1)
    return np.ascontiguousarray(first), np.ascontiguousarray(second)


def kernel(**inputs):
    import concourse.bacc as _bacc
    from concourse.bass_utils import run_bass_kernel_spmd as _run

    nc = _bacc.Bacc("TRN2", target_bir_lowering=False, num_devices=1, dynamic_dma_scratch_size=8192)
    arrays, args = {}, []
    consts, bands = shape_constants()
    given = [(name, np.ascontiguousarray(inputs[name])) for name in _INS]
    for name, a in given + [("shape_consts", consts), ("band_consts", bands)]:
        arrays[f"in_{name}"] = a
        args.append(nc.dram_tensor(f"in_{name}", a.shape, mybir.dt.from_np(a.dtype), kind="ExternalInput").ap())
    args.append(nc.dram_tensor("out_0", (1, SEQ, D_MODEL), F32, kind="ExternalOutput").ap())
    trunk(nc, *args)
    r = _run(nc, [arrays], core_ids=[0])
    return r.results[0]["out_0"]
```

```python
import math
from contextlib import ExitStack

import numpy as np

import concourse.bass as bass
from concourse import mybir

F32 = mybir.dt.float32
F32R = mybir.dt.float32r
I32 = mybir.dt.int32
ALU = mybir.AluOpType
ACT = mybir.ActivationFunctionType

P = 128
D_MODEL = 2048
SEQ = 256
NT = SEQ // P
KT = D_MODEL // P
N_HEADS = 16
LORA = 512
LT = LORA // P
NOPE = 128
ROPE = 64
HALF = ROPE // 2
QK_HEAD = NOPE + ROPE
V_HEAD = 128
GH = 4
GROUPS = N_HEADS // GH
ROPE_THETA = 10000.0
WINDOWS = (2, 4, 8, 16)
D_FF = 4 * D_MODEL
EPS = 1e-6
SCALE = 1.0 / math.sqrt(QK_HEAD)
MASKED = -3.0e38

COLS = 512
RAW_SLOTS = 4
LEAD = 4
SLABS = D_MODEL // COLS
FF_SLABS = D_FF // COLS
FB = COLS // P

U_DQKV = 0
U_ATT = U_DQKV + 2 * KT // 2
U_WO = U_ATT + 8 * GROUPS
U_MLP = (U_WO + SLABS * KT // 2, 0)
U_POOL = U_MLP[0] + 16 * FF_SLABS
U_MLP = (U_MLP[0], U_POOL + 2 * SLABS)
U_END = U_MLP[1] + 16 * FF_SLABS

TURN_BANK = ((0, 2, 0, 6), (0, 2, 0, 4), (4, 6, 4, 6), (0, 2, 0, 4))
S_WO = 0
S_MLP = (SLABS, SLABS + FF_SLABS * SLABS + SLABS)
S_POOL = S_MLP[0] + FF_SLABS * SLABS

S_END = S_MLP[1] + FF_SLABS * SLABS
ADDED_BEFORE = (0, S_WO, S_MLP[0] + (FF_SLABS - 1) * SLABS, S_POOL,
                S_MLP[1] + (FF_SLABS - 1) * SLABS)
SCORE_COLS = ((0, P), (P, 3 * P))

GAIN_COL = (0, 2 * KT, KT, 3 * KT)
Q_GAIN = 4 * KT
N_GAINS = 4 * KT + 2 * LT

TWO_PI_A = 6.28125
TWO_PI_B = float(np.float32(2 * math.pi - TWO_PI_A))
TWO_PI_B = float(np.float32(np.round(TWO_PI_B * 2**20) / 2**20))
TWO_PI_C = float(np.float32(2 * math.pi - TWO_PI_A - TWO_PI_B))
PI_IN = 3.1415925
ROUNDER = 1.5 * 2.0**23


def trunk(nc, x, positions, ln_mix, ln_mlp, w_dqkv, q_norm, kv_norm, w_uq, w_ukv, w_o,
          w_pool, pool_scale, w_up, w_down, final_norm, shape_consts, band_consts, out):
    ctx = ExitStack()
    with ctx:
        def sb(name, shape, dt=F32):
            return ctx.enter_context(nc.sbuf_tensor(name, shape, dt))

        def sem(name):
            return ctx.enter_context(nc.semaphore(name))

        resid = sb("resid", [P, NT, D_MODEL])
        weight_raw = sb("weight_raw", [P, RAW_SLOTS, 4, COLS])
        weight_hi = sb("weight_hi", [P, LEAD, 2, COLS], F32R)
        weight_lo = sb("weight_lo", [P, LEAD, 2, COLS], F32R)
        xt = sb("xt", [P, KT, 2 * SEQ], F32R)
        xt2 = sb("xt2", [P, KT, 2 * SEQ], F32R)
        mid = sb("mid", [P, 2, FB, 2 * SEQ], F32R)
        scratch = sb("scratch", [P, 2 * D_MODEL])
        row_gain = sb("row_gain", [P, D_MODEL])
        early = sb("early", [P, 1536])
        p_t = sb("p_t", [P, GH, 6 * P], F32R)
        cos_t = sb("cos_t", [P, 2, SEQ])
        sin_t = sb("sin_t", [P, 2, SEQ])
        consts = sb("consts", [P, 3 * P + 1])
        gain_col = sb("gain_col", [P, N_GAINS])
        small = sb("small", [P, 96])
        ps = ctx.enter_context(nc.psum_tensor("ps", [P, 8, COLS], F32))

        ident = consts[:, 0:P]
        causal = consts[:, P:3 * P]
        inv_freq = consts[:, 3 * P:3 * P + 1]
        latent_t = mid[:, :, :, :].rearrange("p a b c -> p (a b) c")
        q_t = xt2[:, 0:4, :]
        k_t = xt2[:, 4:8, :]
        v_hi = xt2[:, 8:10, :]
        v_lo = xt2[:, 10:12, :]
        qr_t = xt2[:, 12:14, :]
        kr_t = xt2[:, 14:16, :]
        turned_into = (xt, xt2, xt, xt2)
        latent = scratch[:, 0:2 * NT * LORA].rearrange("p (t n) -> p t n", t=NT)
        tail_raw = early[:, 0:KT * ROPE].rearrange("p (k c) -> p k c", k=KT)
        tail_hi = q_t[:, 0:2, :].rearrange("p a (k c) -> p (a k) c", c=ROPE)
        tail_lo = q_t[:, 2:4, :].rearrange("p a (k c) -> p (a k) c", c=ROPE)
        k_rope = early[:, KT * ROPE:KT * ROPE + 512].rearrange("p (t a r j) -> p t a r j", t=NT, a=2, r=4)
        pos_i = early[:, 8 * P:8 * P + SEQ].bitcast(I32)
        gain_rows = early[0:N_GAINS, 11 * P:12 * P]
        probs = early[:, :].rearrange("p (h c) -> p h c", h=GH)
        bands = early[:, :].rearrange("p (g c) -> p g c", g=SLABS)
        fold_b = [scratch[:, s * 1024:(s + 1) * 1024].rearrange("p (b n) -> p b n", b=FB) for s in (0, 1)]
        fold_s = [scratch[:, s * 1024:(s + 1) * 1024].rearrange("p (b n) -> p b n", b=FB) for s in (2, 3)]
        rot_b = scratch[:, 1024:1536].rearrange("p (a n) -> p a n", a=2)
        rot_x = scratch[:, 1536:2048].rearrange("p (a n) -> p a n", a=2)
        rot_c = scratch[:, 3072:3584].rearrange("p (a n) -> p a n", a=2)
        rot_s = scratch[:, 3584:4096].rearrange("p (a n) -> p a n", a=2)
        squares_out = scratch[:, 1024:2048].rearrange("p (t n) -> p t n", t=NT)
        pool_gained = scratch[:, 0:1024].rearrange("p (t n) -> p t n", t=NT)
        pool_sums = [scratch[:, s * 1024:(s + 1) * 1024].rearrange("p (t n) -> p t n", t=NT) for s in (2, 3)]
        result = scratch[:, :].rearrange("p (t n) -> p t n", t=NT)
        sumsq = small[:, 0:8].rearrange("p (t s) -> p t s", t=NT)
        total = small[:, 8:10]
        root = small[:, 10:12]
        rstd = small[:, 12:14]
        rstd_sq = small[:, 14:16]
        eps = small[:, 16:17]
        c_sumsq = small[:, 20:24].rearrange("p (j t) -> p j t", j=2)
        c_root = small[:, 24:28].rearrange("p (j t) -> p j t", j=2)
        c_rstd = small[:, 28:32].rearrange("p (j t) -> p j t", j=2)
        c_scale = small[:, 32:36].rearrange("p (j t) -> p j t", j=2)
        row_max = small[:, 40:48]
        neg_max = small[:, 48:56]
        row_sum = small[:, 56:64]
        inv_sum = small[:, 64:72]
        step_mark = small[:, 72:74]

        x_in = [sem(f"x_in{s}") for s in range(SLABS)]
        consts_in, gains_in, pos_in, tail_in = sem("consts_in"), sem("gains_in"), sem("pos_in"), sem("tail_in")
        band_in, scale_in, final_in, out_done = sem("band_in"), sem("scale_in"), sem("final_in"), sem("out_done")
        raw_in = [sem(f"raw_in{s}") for s in range(RAW_SLOTS)]
        hi_made, lo_made, unit_used = sem("hi_made"), sem("lo_made"), sem("unit_used")
        gains_turned, gains_ready, eps_set = sem("gains_turned"), sem("gains_ready"), sem("eps_set")
        squared, totalled, rooted, rstd_made = sem("squared"), sem("totalled"), sem("rooted"), sem("rstd_made")
        mean_made, rstd_sq_made = sem("mean_made"), sem("rstd_sq_made")
        turned, xt_hi_made, xt_made = sem("turned"), sem("xt_hi_made"), sem("xt_made")
        slab_read, bands_scaled = sem("slab_read"), sem("bands_scaled")
        pool_copied, pooled, pool_scaled = sem("pool_copied"), sem("pooled"), sem("pool_scaled")
        up_low, up_summed = sem("up_low"), sem("up_summed")
        up_squared, up_hi, up_made = sem("up_squared"), sem("up_hi"), sem("up_made")
        tail_hi_made, tail_made = sem("tail_hi_made"), sem("tail_made")
        tail_done, c_squared, c_rooted, c_rstd_made = sem("tail_done"), sem("c_squared"), sem("c_rooted"), sem("c_rstd_made")
        c_scale_made = sem("c_scale_made")
        c_scaled, c_turned, ct_hi_made, ct_made = sem("c_scaled"), sem("c_turned"), sem("ct_hi_made"), sem("ct_made")
        kr_copied, kr_turned = sem("kr_copied"), sem("kr_turned")
        table_step, angles_made, tables_made = sem("table_step"), sem("angles_made"), sem("tables_made")
        rot_low, rot_step, rot_made, rot_hi, rotated = (sem("rot_low"), sem("rot_step"), sem("rot_made"),
                                                        sem("rot_hi"), sem("rotated"))
        r_summed = sem("r_summed")
        q_low, q_summed, q_hi, q_made = sem("q_low"), sem("q_summed"), sem("q_hi"), sem("q_made")
        k_low, k_summed, k_hi, k_made = sem("k_low"), sem("k_summed"), sem("k_hi"), sem("k_made")
        v_hi_made, v_made = sem("v_hi_made"), sem("v_made")
        scores_done, scores_masked, neg_max_made = sem("scores_done"), sem("scores_masked"), sem("neg_max_made")
        exp_made, inv_made, probs_made = sem("exp_made"), sem("inv_made"), sem("probs_made")
        probs_turned, pt_hi_made, pt_made = sem("probs_turned"), sem("pt_hi_made"), sem("pt_made")
        o_done, o_low, o_summed, o_hi, o_made = (sem("o_done"), sem("o_low"), sem("o_summed"),
                                                 sem("o_hi"), sem("o_made"))
        gained, final_t0, final_t1 = sem("gained"), sem("final_t0"), sem("final_t1")

        block = ctx.enter_context(nc.Block())

        @block.sync
        def _(sp):
            def load(c, source, dyn=0, width=COLS):
                if c >= RAW_SLOTS:
                    sp.wait_ge(lo_made, 2 * (c - RAW_SLOTS) + 2 + dyn)
                sp.dma_start(weight_raw[:, c % RAW_SLOTS, :, 0:width], source).then_inc(raw_in[c % RAW_SLOTS], 16)

            def rows(w, first, n=4):
                return w[first:first + n * P, :].rearrange("(k p) n -> p k n", p=P)

            sp.dma_start(consts[:, :], shape_consts).then_inc(consts_in, 16)
            for slab in range(2):
                for c in range(4):
                    if slab == 0:
                        cols = slice(c * COLS, (c + 1) * COLS)
                        sp.dma_start(resid[:, :, cols], x[0].rearrange("(t p) n -> p t n", p=P)[:, :, cols]
                                     ).then_inc(x_in[c], 16)
                    if slab == 0 and c == 0:
                        first = 0
                        for g in (ln_mix, ln_mlp, q_norm, kv_norm):
                            n = g.shape[0] * g.shape[1] // P
                            sp.dma_start(gain_rows[first:first + n, :],
                                         g.rearrange("l (k p) -> (l k) p", p=P)).then_inc(gains_in, 16)
                            first += n
                    load(U_DQKV // 2 + 4 * slab + c,
                         rows(w_dqkv[0], 4 * P * c)[:, :, slab * COLS:(slab + 1) * COLS])
            sp.dma_start(tail_raw, w_dqkv[0, :, 2 * LORA:2 * LORA + ROPE]
                         .rearrange("(k p) n -> p k n", p=P)).then_inc(tail_in, 16)
            uq = rows(w_uq[0], 0).rearrange("p k (h c) -> p k h c", h=N_HEADS)
            ukv = rows(w_ukv[0], 0).rearrange("p k (h c) -> p k h c", h=N_HEADS)

            def load_heads(c, w, h0, c0, width, dyn, h_dyn):
                if c >= RAW_SLOTS:
                    sp.wait_ge(lo_made, 2 * (c - RAW_SLOTS) + 2 + dyn)
                for k in range(LT):
                    dst = weight_raw[:, c % RAW_SLOTS, k, 0:GH * width].rearrange("p (h c) -> p h c", h=GH)
                    sp.dma_start(dst, w[:, k, bass.ds(h_dyn + h0, GH), c0:c0 + width]).then_inc(
                        raw_in[c % RAW_SLOTS], 16)

            def load_group(c, dyn, h_dyn):
                load_heads(c, uq, 0, 0, NOPE, dyn, h_dyn)
                load_heads(c + 1, ukv, 0, 0, NOPE, dyn, h_dyn)
                load_heads(c + 2, uq, 0, NOPE, ROPE, dyn, h_dyn)
                load_heads(c + 3, ukv, 0, NOPE, V_HEAD, dyn, h_dyn)

            with sp.Fori(0, GROUPS) as g:
                load_group(U_ATT // 2, g * 8, g * GH)
            for slab in range(SLABS):
                for c in range(4):
                    load(U_WO // 2 + 4 * slab + c, rows(w_o[0], 4 * P * c)[:, :, slab * COLS:(slab + 1) * COLS])

            def load_up(layer, c, s, dyn=0):
                for j in range(4):
                    load(c + j, w_up[layer, 4 * P * j:4 * P * (j + 1), bass.ds(s * COLS, COLS)]
                         .rearrange("(k p) n -> p k n", p=P), dyn)

            def load_down(layer, c, s, dyn=0):
                for n in range(SLABS):
                    load(c + n, w_down[layer, bass.ds(s * COLS, COLS), n * COLS:(n + 1) * COLS]
                         .rearrange("(k p) n -> p k n", p=P), dyn)

            def load_mlp(layer):
                c = U_MLP[layer] // 2
                load_up(layer, c, 0)
                with sp.Fori(0, FF_SLABS // 2 - 1) as i:
                    load_up(layer, c + 4, i * 2 + 1, i * 32)
                    load_down(layer, c + 8, i * 2, i * 32)
                    load_up(layer, c + 12, i * 2 + 2, i * 32)
                    load_down(layer, c + 16, i * 2 + 1, i * 32)
                last = c + 4 + 16 * (FF_SLABS // 2 - 1)
                load_up(layer, last, FF_SLABS - 1)
                load_down(layer, last + 4, FF_SLABS - 2)
                load_down(layer, last + 8, FF_SLABS - 1)

            load_mlp(0)
            for g in range(SLABS):
                load(U_POOL // 2 + g, rows(w_pool[0, g], 0))
            load_mlp(1)
            for half in range(2):
                cols = slice(half * D_MODEL // 2, (half + 1) * D_MODEL // 2)
                for t, made in enumerate((final_t0, final_t1)):
                    sp.wait_ge(made, half + 1)
                    sp.dma_start(out[0, t * P:(t + 1) * P, cols], result[:, t, cols]).then_inc(out_done, 16)
            sp.wait_ge(out_done, 16 * 2 * NT)

        @block.gpsimd
        def _(pool):
            pool.dma_start(pos_i, positions.to_broadcast([P, SEQ])).then_inc(pos_in, 16)
            pool.dma_start(row_gain[:, :], pool_scale.to_broadcast([P, D_MODEL])).then_inc(scale_in, 16)
            pool.wait_ge(probs_turned, GROUPS)
            pool.dma_start(early[:, :], band_consts).then_inc(band_in, 16)
            pool.wait_ge(slab_read, S_POOL + SLABS)
            pool.dma_start(row_gain[:, :], final_norm.rearrange("(a n) -> a n", a=1)
                           .to_broadcast([P, D_MODEL])).then_inc(final_in, 16)
            pool.wait_ge(final_in, 16)
            for s in range(SLABS - 1):
                pool.wait_ge(squared, NT * (4 * SLABS + s + 1))
                for t in range(NT):
                    cols = resid[:, t, s * COLS:(s + 1) * COLS]
                    nc.gpsimd.tensor_tensor(cols, cols, row_gain[:, s * COLS:(s + 1) * COLS],
                                            ALU.mult).then_inc(gained, 1)

        def raw_of(v):
            return weight_raw[:, (v // 2) % RAW_SLOTS, 2 * (v % 2):2 * (v % 2) + 2, :]

        def raw_ready(v):
            c = v // 2
            per = lambda j: 16 * LT if U_ATT // 2 <= j < U_WO // 2 else 16
            return sum(per(j) for j in range(c % RAW_SLOTS, c + 1, RAW_SLOTS))

        def rope_views(dst, v, raw):
            for a in range(2):
                yield (dst[:, v % LEAD, :, a * P:(a + 1) * P].rearrange("p k (h j) -> p k h j", h=GH),
                       raw[:, :, 0:GH * ROPE].rearrange("p k (h a j) -> p k a h j", h=GH, a=2)[:, :, a])

        def is_rope(v):
            return U_ATT <= v < U_WO and (v - U_ATT) % 8 in (4, 5)

        @block.scalar
        def _(act):
            def split(v, dyn=0, raw_dyn=0):
                if v >= U_END:
                    return
                act.wait_ge(raw_in[(v // 2) % RAW_SLOTS], raw_ready(v) + raw_dyn)
                if v >= LEAD:
                    act.wait_ge(unit_used, v - LEAD + 1 + dyn)
                if is_rope(v):
                    for dst, src in rope_views(weight_hi, v, raw_of(v)):
                        last = nc.scalar.copy(dst, src)
                else:
                    last = nc.scalar.copy(weight_hi[:, v % LEAD, :, :], raw_of(v))
                last.then_inc(hi_made, 1)

            def position(k, dyn=0, raw_dyn=0):
                split(k + LEAD, dyn, raw_dyn)

            def squares(n, s):
                if n == 0:
                    act.wait_ge(x_in[s], 16)
                else:
                    act.wait_ge(slab_read, ADDED_BEFORE[n] + s + 1)
                if n + s > 0:
                    act.wait_ge(squared, NT * (SLABS * n + s))
                if n > 0 and s == 0:
                    act.wait_ge(totalled, n)
                for t in range(NT):
                    nc.scalar.activation(squares_out[:, t, :], resid[:, t, s * COLS:(s + 1) * COLS], ACT.Square,
                                         accum_out=sumsq[:, t, s:s + 1]).then_inc(squared, 1)

            def root_of_mean(i, n):
                act.wait_ge(totalled, n + 1)
                nc.scalar.activation(root, total, ACT.Sqrt, bias=eps, scale=1.0 / D_MODEL).then_inc(rooted, 1)

            def turn_hi(n, s):
                for k in range(4 * s, 4 * s + 4):
                    act.wait_ge(turned, 8 * n + k // 2 + 1)
                    bank = TURN_BANK[n][s] + k // 2 % 2
                    g = GAIN_COL[n] + k
                    nc.scalar.activation(turned_into[n][:, k, 0:SEQ], ps[:, bank, (k % 2) * SEQ:(k % 2 + 1) * SEQ],
                                         ACT.Copy, scale=gain_col[:, g:g + 1]).then_inc(xt_hi_made, 1)

            def c_norm_start(j):
                act.wait_ge(unit_used, U_DQKV + 8 * (j + 1))
                for t in range(NT):
                    nc.scalar.activation(latent[:, t, j * LORA:(j + 1) * LORA], ps[:, 4 + 2 * j + t, :], ACT.Square,
                                         scale=rstd[:, t:t + 1], accum_out=c_sumsq[:, j, t:t + 1]).then_inc(c_squared, 1)
                act.wait_ge(c_squared, 2 * j + 2)
                nc.scalar.activation(c_root[:, j, :], c_sumsq[:, j, :], ACT.Sqrt, bias=eps,
                                     scale=1.0 / LORA).then_inc(c_rooted, 1)
                act.wait_ge(c_scale_made, j + 1)
                for t in range(NT):
                    nc.scalar.activation(latent[:, t, j * LORA:(j + 1) * LORA], ps[:, 4 + 2 * j + t, :], ACT.Copy,
                                         scale=c_scale[:, j, t:t + 1]).then_inc(c_scaled, 1)

            def c_round(j):
                for k in range(LT):
                    act.wait_ge(c_turned, 2 * j + k // 2 + 1)
                    g = Q_GAIN + j * LT + k
                    nc.scalar.activation(latent_t[:, j * LT + k, 0:SEQ],
                                         ps[:, 6 * j + k // 2, (k % 2) * SEQ:(k % 2 + 1) * SEQ], ACT.Copy,
                                         scale=gain_col[:, g:g + 1]).then_inc(ct_hi_made, 1)

            def fold_low(k, dyn, low, side):
                act.wait_ge(unit_used, k + 1 + dyn)
                nc.scalar.copy(fold_b[side], ps[:, 4 * side:4 * side + 4, SEQ:2 * SEQ]).then_inc(low, 1)

            def round_hi(n, dyn, value_made, dst, value, hi):
                act.wait_ge(value_made, n + 1 + dyn)
                nc.scalar.copy(dst, value).then_inc(hi, 1)

            act.wait_ge(gains_turned, 1)
            nc.scalar.copy(gain_col[:, :], ps[:, 7, 0:N_GAINS]).then_inc(gains_ready, 1)
            act.wait_ge(gains_ready, 1)
            for s in range(SLABS):
                turn_hi(0, s)
                split(2 * s)
                split(2 * s + 1)
                squares(0, s)
            act.wait_ge(eps_set, 1)
            root_of_mean(0, 0)
            for k in range(U_DQKV + 4, U_ATT):
                position(k)
                if k == 5:
                    act.wait_ge(tail_in, 16)
                    nc.scalar.copy(tail_hi, tail_raw).then_inc(tail_hi_made, 1)
                if k == 6:
                    act.wait_ge(angles_made, 1)
                    for a in range(2):
                        nc.scalar.activation(sin_t[:, a, :], rot_c[:, 0, :], ACT.Sin).then_inc(tables_made, 1)
                        nc.scalar.activation(cos_t[:, a, :], rot_c[:, 1, :], ACT.Sin).then_inc(tables_made, 1)
                if k == 7:
                    act.wait_ge(rstd_made, 1)
                    c_norm_start(0)
                    c_round(0)
            c_norm_start(1)
            act.wait_ge(tail_done, 1)
            for t in range(NT):
                for r in range(4):
                    last = nc.scalar.activation(k_rope[:, t, :, r, :],
                                                ps[:, 4 + t, 0:ROPE].rearrange("p (a j) -> p a j", a=2),
                                                ACT.Copy, scale=rstd[:, t:t + 1])
            last.then_inc(kr_copied, 1)
            c_round(1)
            round_hi(0, 0, rot_made, kr_t[:, :, 0:SEQ], rot_x, rot_hi)

            def q_low_part(g, dyn=0):
                fold_low(U_ATT + 8 * g + 1, dyn * 8, q_low, 0)

            def q_round(g, dyn=0):
                round_hi(g, dyn, q_summed, q_t[:, :, 0:SEQ], fold_s[0], q_hi)

            def k_low_part(g, dyn=0):
                fold_low(U_ATT + 8 * g + 3, dyn * 8, k_low, 1)

            def k_round(g, dyn=0):
                round_hi(g, dyn, k_summed, k_t[:, :, 0:SEQ], fold_s[1], k_hi)

            def r_low_part(g, dyn=0):
                act.wait_ge(unit_used, U_ATT + 8 * g + 6 + dyn * 8)
                nc.scalar.copy(rot_b, ps[:, 4:6, SEQ:2 * SEQ]).then_inc(rot_low, 1)

            def r_round(g, dyn=0):
                round_hi(g + 1, dyn, rot_made, qr_t[:, :, 0:SEQ], rot_x, rot_hi)

            def v_round(g, dyn=0):
                act.wait_ge(unit_used, U_ATT + 8 * g + 8 + dyn * 8)
                nc.scalar.copy(v_hi[:, :, :], ps[:, 6:8, :]).then_inc(v_hi_made, 1)

            def exps(g, dyn=0):
                act.wait_ge(neg_max_made, g + 1 + dyn)
                for h in range(GH):
                    for t in range(NT):
                        i = NT * h + t
                        part = probs[:, h, SCORE_COLS[t][0]:SCORE_COLS[t][1]]
                        nc.scalar.activation(part, part, ACT.Exp, bias=neg_max[:, i:i + 1], scale=SCALE,
                                             accum_out=row_sum[:, i:i + 1]).then_inc(exp_made, 1)

            def pt_round(g, dyn=0):
                act.wait_ge(probs_turned, g + 1 + dyn)
                nc.scalar.copy(p_t[:, :, 0:2 * P], ps[:, 0:4, 0:2 * P]).then_inc(pt_hi_made, 1)
                nc.scalar.copy(p_t[:, :, 4 * P:5 * P], ps[:, 0:4, 2 * P:3 * P]).then_inc(pt_hi_made, 1)

            def o_low_part(g, dyn=0):
                act.wait_ge(o_done, g + 1 + dyn)
                nc.scalar.copy(fold_b[0], ps[:, 0:4, SEQ:2 * SEQ]).then_inc(o_low, 1)

            def o_round(g, dyn=0):
                act.wait_ge(o_summed, g + 1 + dyn)
                nc.scalar.copy(xt[:, bass.ds(dyn * GH + g * GH, GH), 0:SEQ], fold_s[0]).then_inc(o_hi, 1)

            def attention_step(g, i=0):
                b, dyn, raw_dyn = U_ATT + 8 * (g + 1), i * 8, i * 16 * LT
                if g >= 0:
                    exps(g, i)
                position(b, dyn, raw_dyn)
                q_low_part(g + 1, i)
                position(b + 1, dyn, raw_dyn)
                q_round(g + 1, i)
                position(b + 2, dyn, raw_dyn)
                k_low_part(g + 1, i)
                position(b + 3, dyn, raw_dyn)
                k_round(g + 1, i)
                if g >= 0:
                    pt_round(g, i)
                position(b + 4, dyn, raw_dyn)
                r_low_part(g + 1, i)
                position(b + 5, dyn, raw_dyn)
                r_round(g + 1, i)
                if g >= 0:
                    o_low_part(g, i)
                position(b + 6, dyn, raw_dyn)
                if g >= 0:
                    o_round(g, i)
                v_round(g + 1, i)
                position(b + 7, dyn, raw_dyn)

            attention_step(-1)
            with act.Fori(0, GROUPS - 2) as i:
                attention_step(0, i)
            attention_step(GROUPS - 2)
            exps(GROUPS - 1)
            pt_round(GROUPS - 1)
            o_low_part(GROUPS - 1)
            o_round(GROUPS - 1)

            for k in range(U_WO, U_MLP[0]):
                position(k)
                if (k - U_WO) % 8 == 7 and k - U_WO > 7:
                    squares(1, (k - U_WO) // 8 - 1)
                    turn_hi(1, (k - U_WO) // 8 - 1)

            def mlp(layer, norm_index):
                s0 = layer * FF_SLABS

                def up(b, s, dyn=0, raw_dyn=0):
                    side = 0 if s == 0 else 1
                    for k in range(8):
                        position(b + k, dyn, raw_dyn)
                        if s == 0 and k == 1:
                            squares(norm_index, SLABS - 1)
                            turn_hi(norm_index, SLABS - 1)
                    act.wait_ge(unit_used, b + 8 + dyn)
                    nc.scalar.copy(fold_b[0], ps[:, 4 * side:4 * side + 4, SEQ:2 * SEQ]).then_inc(up_low, 1)

                def square_hi(s, s_dyn=0):
                    round_hi(s0 + s, s_dyn, up_squared, mid[:, s % 2, :, 0:SEQ], fold_s[1], up_hi)

                def down(b, s_up, dyn=0, raw_dyn=0, s_dyn=0):
                    for k in range(8):
                        position(b + k, dyn, raw_dyn)
                        if s_up is not None and k == 1:
                            square_hi(s_up, s_dyn)
                        if s_up is None and k % 2 == 1 and k > 1:
                            squares(norm_index + 1, k // 2 - 1)
                            if layer == 0:
                                turn_hi(norm_index + 1, k // 2 - 1)

                b = U_MLP[layer]
                up(b, 0)
                square_hi(0)
                with act.Fori(0, FF_SLABS // 2 - 1) as i:
                    up(b + 8, 1, i * 32, i * 64)
                    down(b + 16, 1, i * 32, i * 64, i * 2)
                    up(b + 24, 2, i * 32, i * 64)
                    down(b + 32, 2, i * 32, i * 64, i * 2)
                b = U_MLP[layer] + 16 * FF_SLABS - 24
                up(b, FF_SLABS - 1)
                down(b + 8, FF_SLABS - 1)
                down(b + 16, None)

            mlp(0, 1)
            squares(2, SLABS - 1)
            root_of_mean(1, 2)
            for k in range(U_POOL, U_MLP[1]):
                position(k)
                g = (k - U_POOL) // 2
                if k == U_POOL + 1:
                    turn_hi(2, SLABS - 1)
                if k % 2 == 1:
                    act.wait_ge(unit_used, k + 1)
                    if g >= 2:
                        act.wait_ge(pooled, g - 1)
                    nc.scalar.copy(pool_sums[g % 2], ps[:, 2 * (g % 2):2 * (g % 2) + 2, :]).then_inc(pool_copied, 1)
            for s in range(SLABS - 1):
                squares(3, s)
                turn_hi(3, s)
            mlp(1, 3)
            squares(4, SLABS - 1)
            root_of_mean(2, 4)
            act.wait_ge(rstd_made, 3)
            act.wait_ge(gained, NT * SLABS)
            for half in range(2):
                cols = slice(half * D_MODEL // 2, (half + 1) * D_MODEL // 2)
                nc.scalar.activation(result[:, 0, cols], resid[:, 0, cols], ACT.Copy,
                                     scale=rstd[:, 0:1]).then_inc(final_t0, 1)

        @block.vector
        def _(dve):
            def as_f32(a):
                return a.bitcast(F32)

            def split(v, dyn=0):
                if v >= U_END:
                    return
                dve.wait_ge(hi_made, v + 1 + dyn)
                if is_rope(v):
                    for (dst, src), (hi, _) in zip(rope_views(weight_lo, v, raw_of(v)),
                                                   rope_views(weight_hi, v, raw_of(v))):
                        last = nc.vector.tensor_tensor(dst, src, as_f32(hi), ALU.subtract)
                else:
                    last = nc.vector.tensor_tensor(weight_lo[:, v % LEAD, :, :], raw_of(v),
                                                   as_f32(weight_hi[:, v % LEAD, :, :]), ALU.subtract)
                last.then_inc(lo_made, 1)

            def position(k, dyn=0):
                split(k + LEAD, dyn)

            def mean_square(n):
                dve.wait_ge(squared, NT * SLABS * (n + 1))
                nc.vector.reduce_sum(total, sumsq, mybir.AxisListType.X).then_inc(totalled, 1)

            def make_rstd(i, n):
                mean_square(n)
                dve.wait_ge(rooted, i + 1)
                nc.vector.reciprocal(rstd, root).then_inc(rstd_made, 1)

            def make_rstd_sq(i, n):
                mean_square(n)
                dve.wait_ge(totalled, n + 1)
                nc.vector.tensor_scalar(rstd_sq, total, 1.0 / D_MODEL, EPS, ALU.mult, ALU.add).then_inc(mean_made, 1)
                dve.wait_ge(mean_made, i + 1)
                nc.vector.reciprocal(rstd_sq, rstd_sq).then_inc(rstd_sq_made, 1)
                dve.wait_ge(rstd_sq_made, i + 1)

            def turn_lo(n, s):
                for k in range(4 * s, 4 * s + 4):
                    dve.wait_ge(xt_hi_made, KT * n + k // 2 * 2 + 2)
                    bank = TURN_BANK[n][s] + k // 2 % 2
                    g = GAIN_COL[n] + k
                    nc.vector.scalar_tensor_tensor(
                        out=turned_into[n][:, k, SEQ:2 * SEQ], in0=ps[:, bank, (k % 2) * SEQ:(k % 2 + 1) * SEQ],
                        scalar=gain_col[:, g:g + 1], in1=as_f32(turned_into[n][:, k, 0:SEQ]),
                        op0=ALU.mult, op1=ALU.subtract).then_inc(xt_made, 1)

            def c_norm(j):
                dve.wait_ge(c_rooted, j + 1)
                nc.vector.reciprocal(c_rstd[:, j, :], c_root[:, j, :]).then_inc(c_rstd_made, 1)
                dve.wait_ge(c_rstd_made, j + 1)
                nc.vector.tensor_tensor(c_scale[:, j, :], c_rstd[:, j, :], rstd, ALU.mult).then_inc(c_scale_made, 1)
                for k in range(LT):
                    dve.wait_ge(ct_hi_made, LT * j + k // 2 * 2 + 2)
                    g = Q_GAIN + j * LT + k
                    nc.vector.scalar_tensor_tensor(
                        out=latent_t[:, j * LT + k, SEQ:2 * SEQ],
                        in0=ps[:, 6 * j + k // 2, (k % 2) * SEQ:(k % 2 + 1) * SEQ],
                        scalar=gain_col[:, g:g + 1], in1=as_f32(latent_t[:, j * LT + k, 0:SEQ]),
                        op0=ALU.mult, op1=ALU.subtract).then_inc(ct_made, 1)

            def rope_angles():
                steps = [0]

                def then_wait(instruction):
                    steps[0] += 1
                    instruction.then_inc(table_step, 1)
                    dve.wait_ge(table_step, steps[0])

                angle, turns, r = rot_s[:, 0, :], rot_s[:, 1, :], rot_c[:, 0, :]
                shifted, wrap = rot_c[:, 1, :], rot_s[:, 0, :]
                dve.wait_ge(pos_in, 16)
                dve.wait_ge(consts_in, 16)
                then_wait(nc.vector.tensor_copy(turns, pos_i))
                then_wait(nc.vector.tensor_scalar(angle, turns, inv_freq, None, ALU.mult))
                then_wait(nc.vector.tensor_scalar(turns, angle, 0.5 / math.pi, ROUNDER, ALU.mult, ALU.add))
                then_wait(nc.vector.tensor_scalar(turns, turns, ROUNDER, None, ALU.subtract))
                then_wait(nc.vector.scalar_tensor_tensor(out=r, in0=turns, scalar=-TWO_PI_A, in1=angle,
                                                         op0=ALU.mult, op1=ALU.add))
                for part in (TWO_PI_B, TWO_PI_C):
                    then_wait(nc.vector.scalar_tensor_tensor(out=r, in0=turns, scalar=-part, in1=r,
                                                             op0=ALU.mult, op1=ALU.add))
                then_wait(nc.vector.tensor_scalar(shifted, r, 0.5 * math.pi, None, ALU.add))
                then_wait(nc.vector.tensor_scalar(wrap, shifted, math.pi, -2.0 * math.pi, ALU.is_gt, ALU.mult))
                then_wait(nc.vector.tensor_tensor(shifted, shifted, wrap, ALU.add))
                nc.vector.tensor_scalar(rot_c, rot_c, PI_IN, -PI_IN, ALU.min, ALU.max).then_inc(angles_made, 1)

            def rotate(n, source, dst, dyn=0):
                if n >= 1:
                    dve.wait_ge(rot_made, n + dyn)
                nc.vector.tensor_tensor(rot_c, source, cos_t[:, :, :], ALU.mult).then_inc(rot_step, 1)
                nc.vector.tensor_tensor(rot_s, source, sin_t[:, :, :], ALU.mult).then_inc(rot_step, 1)
                dve.wait_ge(rot_step, 2 * n + 2 + 2 * dyn)
                nc.vector.tensor_tensor(rot_x[:, 0, :], rot_c[:, 0, :], rot_s[:, 1, :], ALU.subtract)
                nc.vector.tensor_tensor(rot_x[:, 1, :], rot_c[:, 1, :], rot_s[:, 0, :],
                                        ALU.add).then_inc(rot_made, 1)
                dve.wait_ge(rot_hi, n + 1 + dyn)
                nc.vector.tensor_tensor(dst[:, :, SEQ:2 * SEQ], rot_x, as_f32(dst[:, :, 0:SEQ]),
                                        ALU.subtract).then_inc(rotated, 1)

            def fold_sum(n, dyn, low, summed, side):
                dve.wait_ge(low, n + 1 + dyn)
                nc.vector.tensor_tensor(fold_s[side], ps[:, 4 * side:4 * side + 4, 0:SEQ], fold_b[side],
                                        ALU.add).then_inc(summed, 1)

            def subtract_hi(n, dyn, value, dst, hi, made):
                dve.wait_ge(hi, n + 1 + dyn)
                nc.vector.tensor_tensor(dst[:, :, SEQ:2 * SEQ], value, as_f32(dst[:, :, 0:SEQ]),
                                        ALU.subtract).then_inc(made, 1)

            def r_sum(g, dyn=0):
                dve.wait_ge(rot_low, g + 1 + dyn)
                nc.vector.tensor_tensor(rot_x, ps[:, 4:6, 0:SEQ], rot_b, ALU.add).then_inc(r_summed, 1)
                dve.wait_ge(r_summed, g + 1 + dyn)

            def v_low(g, dyn=0):
                dve.wait_ge(v_hi_made, g + 1 + dyn)
                nc.vector.tensor_tensor(v_lo[:, :, :], ps[:, 6:8, :], as_f32(v_hi[:, :, :]),
                                        ALU.subtract).then_inc(v_made, 1)

            def mask_scores(g, dyn=0):
                for h in range(GH):
                    if h % 2 == 0:
                        dve.wait_ge(scores_done, 2 * g + h // 2 + 1 + dyn * 2)
                        nc.vector.memset(step_mark[:, h // 2:h // 2 + 1], 0.0)
                    for t in range(NT):
                        lo, hi = SCORE_COLS[t]
                        i = NT * h + t
                        nc.vector.tensor_tensor_reduce(
                            out=probs[:, h, lo:hi], in0=ps[:, 4 + h, lo:hi], in1=causal[:, (1 - t) * P:2 * P],
                            scale=1.0, scalar=-3.4e38, op0=ALU.add, op1=ALU.max,
                            accum_out=row_max[:, i:i + 1]).then_inc(scores_masked, 1)
                dve.wait_ge(scores_masked, 8 * (g + 1) + dyn * 8)
                nc.vector.tensor_scalar(neg_max, row_max, -SCALE, None, ALU.mult).then_inc(neg_max_made, 1)

            def normalise(g, dyn=0):
                dve.wait_ge(exp_made, 8 * (g + 1) + dyn * 8)
                nc.vector.reciprocal(inv_sum, row_sum).then_inc(inv_made, 1)
                dve.wait_ge(inv_made, g + 1 + dyn)
                for h in range(GH):
                    for t in range(NT):
                        i = NT * h + t
                        part = probs[:, h, SCORE_COLS[t][0]:SCORE_COLS[t][1]]
                        nc.vector.tensor_scalar(part, part, inv_sum[:, i:i + 1], None, ALU.mult).then_inc(probs_made, 1)

            def pt_low(g, dyn=0):
                dve.wait_ge(pt_hi_made, 2 * (g + 1) + dyn * 2)
                nc.vector.tensor_tensor(p_t[:, :, 2 * P:4 * P], ps[:, 0:4, 0:2 * P], as_f32(p_t[:, :, 0:2 * P]),
                                        ALU.subtract).then_inc(pt_made, 1)
                nc.vector.tensor_tensor(p_t[:, :, 5 * P:6 * P], ps[:, 0:4, 2 * P:3 * P],
                                        as_f32(p_t[:, :, 4 * P:5 * P]), ALU.subtract).then_inc(pt_made, 1)

            def o_low_part(g, dyn=0):
                dve.wait_ge(o_hi, g + 1 + dyn)
                heads = xt[:, bass.ds(dyn * GH + g * GH, GH), :]
                nc.vector.tensor_tensor(heads[:, :, SEQ:2 * SEQ], fold_s[0], as_f32(heads[:, :, 0:SEQ]),
                                        ALU.subtract).then_inc(o_made, 1)

            def attention_step(g, i=0):
                b, dyn = U_ATT + 8 * (g + 1), i * 8
                if g >= 0:
                    mask_scores(g, i)
                position(b, dyn)
                fold_sum(g + 1, i, q_low, q_summed, 0)
                if g >= 0:
                    normalise(g, i)
                position(b + 1, dyn)
                subtract_hi(g + 1, i, fold_s[0], q_t, q_hi, q_made)
                position(b + 2, dyn)
                fold_sum(g + 1, i, k_low, k_summed, 1)
                position(b + 3, dyn)
                subtract_hi(g + 1, i, fold_s[1], k_t, k_hi, k_made)
                if g >= 0:
                    pt_low(g, i)
                position(b + 4, dyn)
                r_sum(g + 1, i)
                position(b + 5, dyn)
                rotate(g + 2, rot_x, qr_t, i)
                if g >= 0:
                    fold_sum(g, i, o_low, o_summed, 0)
                position(b + 6, dyn)
                if g >= 0:
                    o_low_part(g, i)
                v_low(g + 1, i)
                position(b + 7, dyn)

            def add_slab(k, s, n, bank, scale=None, dyn=0, s_dyn=0):
                dve.wait_ge(unit_used, k + 1 + dyn)
                if s >= 1:
                    dve.wait_ge(slab_read, s + s_dyn)
                for t in range(NT):
                    cols = resid[:, t, n * COLS:(n + 1) * COLS]
                    sums = ps[:, bank + 2 * (n % 2) + t, :]
                    if scale is None:
                        last = nc.vector.tensor_tensor(cols, sums, cols, ALU.add)
                    else:
                        last = nc.vector.scalar_tensor_tensor(out=cols, in0=sums, scalar=scale[:, t:t + 1],
                                                              in1=cols, op0=ALU.mult, op1=ALU.add)
                last.then_inc(slab_read, 1)

            nc.vector.memset(eps, EPS).then_inc(eps_set, 1)
            for s in range(SLABS):
                if s == 0:
                    dve.wait_ge(gains_ready, 1)
                turn_lo(0, s)
                split(2 * s)
                split(2 * s + 1)
            make_rstd(0, 0)
            for k in range(U_DQKV + 4, U_ATT):
                position(k)
                if k == 4:
                    rope_angles()
                if k == 6:
                    dve.wait_ge(tail_hi_made, 1)
                    nc.vector.tensor_tensor(tail_lo, tail_raw, as_f32(tail_hi), ALU.subtract).then_inc(tail_made, 1)
                if k == 7:
                    dve.wait_ge(rstd_made, 1)
                    c_norm(0)
            c_norm(1)
            dve.wait_ge(kr_turned, 1)
            dve.wait_ge(tables_made, 4)
            rotate(0, ps[:, 4, :].rearrange("p (a n) -> p a n", a=2), kr_t)
            attention_step(-1)
            with dve.Fori(0, GROUPS - 2) as i:
                attention_step(0, i)
            attention_step(GROUPS - 2)
            mask_scores(GROUPS - 1)
            normalise(GROUPS - 1)
            pt_low(GROUPS - 1)
            fold_sum(GROUPS - 1, 0, o_low, o_summed, 0)
            o_low_part(GROUPS - 1)

            for n in range(SLABS):
                for k in range(8):
                    position(U_WO + 8 * n + k)
                add_slab(U_WO + 8 * n + 7, S_WO + n, n, 4)
                if n >= 1:
                    turn_lo(1, n - 1)

            def mlp(layer, norm_index):
                s0 = layer * FF_SLABS

                def up(b, s, dyn=0, s_dyn=0):
                    side = 0 if s == 0 else 1
                    for k in range(8):
                        position(b + k, dyn)
                        if s == 0 and k == 1:
                            turn_lo(norm_index, SLABS - 1)
                            make_rstd_sq(layer, norm_index)
                    dve.wait_ge(up_low, s0 + s + 1 + s_dyn)
                    nc.vector.tensor_tensor(fold_s[0], ps[:, 4 * side:4 * side + 4, 0:SEQ], fold_b[0],
                                            ALU.add).then_inc(up_summed, 1)

                def square(s, s_dyn=0):
                    dve.wait_ge(up_summed, s0 + s + 1 + s_dyn)
                    nc.vector.scalar_tensor_tensor(out=fold_s[1], in0=fold_s[0], scalar=0.0, in1=fold_s[0],
                                                   op0=ALU.max, op1=ALU.mult).then_inc(up_squared, 1)

                def square_low(s, s_dyn=0):
                    subtract_hi(s0 + s, s_dyn, fold_s[1], mid[:, s % 2, :, :], up_hi, up_made)

                def down(b, s, s_up, dyn=0, s_dyn=0):
                    for k in range(8):
                        position(b + k, dyn)
                        if s_up is not None and k == 0:
                            square(s_up, s_dyn)
                        if s_up is not None and k == 2:
                            square_low(s_up, s_dyn)
                        if k % 2 == 1:
                            add_slab(b + k, S_MLP[layer] + s * SLABS + k // 2, k // 2, 0, rstd_sq, dyn,
                                     s_dyn * SLABS)
                        if s_up is None and k % 2 == 1 and k > 1 and layer == 0:
                            turn_lo(norm_index + 1, k // 2 - 1)

                b = U_MLP[layer]
                up(b, 0)
                square(0)
                square_low(0)
                with dve.Fori(0, FF_SLABS // 2 - 1) as i:
                    up(b + 8, 1, i * 32, i * 2)
                    down(b + 16, 0, 1, i * 32, i * 2)
                    up(b + 24, 2, i * 32, i * 2)
                    down(b + 32, 1, 2, i * 32, i * 2)
                b = U_MLP[layer] + 16 * FF_SLABS - 24
                up(b, FF_SLABS - 1)
                down(b + 8, FF_SLABS - 2, FF_SLABS - 1)
                down(b + 16, FF_SLABS - 1, None)

            def add_pooled(g):
                dve.wait_ge(pooled, g + 1)
                if g >= 1:
                    dve.wait_ge(slab_read, S_POOL + g)
                for t in range(NT):
                    nc.vector.tensor_tensor(pool_gained[:, t, :], ps[:, 4 + 2 * (g % 2) + t, :],
                                            row_gain[:, g * COLS:(g + 1) * COLS], ALU.mult).then_inc(pool_scaled, 1)
                dve.wait_ge(pool_scaled, NT * (g + 1))
                cols = resid[:, :, g * COLS:(g + 1) * COLS]
                nc.vector.tensor_tensor(cols, pool_gained, cols, ALU.add).then_inc(slab_read, 1)

            mlp(0, 1)
            dve.wait_ge(band_in, 16)
            dve.wait_ge(scale_in, 16)
            make_rstd(1, 2)
            dve.wait_ge(rstd_made, 2)
            for t, cols in ((0, slice(0, SEQ)), (1, slice(SEQ, SEQ + P))):
                nc.vector.tensor_scalar(bands[:, :, cols], bands[:, :, cols], rstd[:, t:t + 1], None,
                                        ALU.mult).then_inc(bands_scaled, 1)
            for k in range(U_POOL, U_MLP[1]):
                position(k)
                if k == U_POOL + 1:
                    turn_lo(2, SLABS - 1)
                if k % 2 == 1 and k > U_POOL + 1:
                    add_pooled((k - U_POOL) // 2 - 1)
            turn_lo(3, 0)
            add_pooled(SLABS - 1)
            turn_lo(3, 1)
            turn_lo(3, 2)
            mlp(1, 3)
            dve.wait_ge(squared, NT * SLABS * 5)
            dve.wait_ge(final_in, 16)
            last_cols = slice((SLABS - 1) * COLS, SLABS * COLS)
            make_rstd(2, 4)
            for t in range(NT):
                nc.vector.tensor_tensor(resid[:, t, last_cols], resid[:, t, last_cols], row_gain[:, last_cols],
                                        ALU.mult).then_inc(gained, 1)
            dve.wait_ge(rstd_made, 3)
            dve.wait_ge(gained, NT * SLABS)
            for half in range(2):
                cols = slice(half * D_MODEL // 2, (half + 1) * D_MODEL // 2)
                nc.vector.tensor_scalar(result[:, 1, cols], resid[:, 1, cols], rstd[:, 1:2], None,
                                        ALU.mult).then_inc(final_t1, 1)

        @block.tensor
        def _(pe):
            mm = nc.tensor.matmul

            def token_unit(k, source, tile, bank, first, last, dyn=0):
                pe.wait_ge(lo_made, k + 1 + dyn)
                s = k % LEAD
                for j in range(2):
                    for t in range(NT):
                        hi = source[:, tile + j, t * P:(t + 1) * P]
                        lo = source[:, tile + j, SEQ + t * P:SEQ + (t + 1) * P]
                        o = ps[:, bank + t, :]
                        mm(o, hi, weight_hi[:, s, j, :], start=first and j == 0, stop=False)
                        mm(o, hi, weight_lo[:, s, j, :], start=False, stop=False)
                        end = mm(o, lo, weight_hi[:, s, j, :], start=False, stop=last and j == 1)
                end.then_inc(unit_used, 1)

            def weight_unit(k, source, tile, bank, first, last, dyn=0, blocks=FB):
                pe.wait_ge(lo_made, k + 1 + dyn)
                s = k % LEAD
                for j in range(2):
                    for f in range(blocks):
                        w_hi = weight_hi[:, s, j, f * P:(f + 1) * P]
                        w_lo = weight_lo[:, s, j, f * P:(f + 1) * P]
                        both = (w_hi, source[:, tile + j, :], ps[:, bank + f, :])
                        high = (w_lo, source[:, tile + j, 0:SEQ], ps[:, bank + f, 0:SEQ])
                        order = (high, both) if j == 1 else (both, high)
                        for i, (w, m, o) in enumerate(order):
                            end = mm(o, w, m, start=first and j == 0 and i == 0, stop=last and j == 1 and i == 1)
                end.then_inc(unit_used, 1)

            def turn(n, s):
                if n == 0:
                    pe.wait_ge(x_in[s], 16)
                else:
                    pe.wait_ge(slab_read, ADDED_BEFORE[n] + s + 1)
                if s == 2:
                    xt_ready(n, 3)
                if n == 2 and s == 3:
                    xt_ready(n, 7)
                for b in range(2):
                    for a in range(2):
                        f = s * COLS + (2 * b + a) * P
                        for t in range(NT):
                            end = nc.tensor.transpose(
                                ps[:, TURN_BANK[n][s] + b, a * SEQ + t * P:a * SEQ + (t + 1) * P],
                                resid[:, t, f:f + P], ident)
                    end.then_inc(turned, 1)

            def xt_ready(n, k):
                pe.wait_ge(xt_made, KT * n + k + 1)

            def c_turn(j):
                pe.wait_ge(c_scaled, NT * (j + 1))
                for b in range(2):
                    for a in range(2):
                        for t in range(NT):
                            f = j * LORA + (2 * b + a) * P
                            end = nc.tensor.transpose(ps[:, 6 * j + b, a * SEQ + t * P:a * SEQ + (t + 1) * P],
                                                      latent[:, t, f:f + P], ident)
                    end.then_inc(c_turned, 1)

            pe.wait_ge(consts_in, 16)
            turn(0, 0)
            pe.wait_ge(gains_in, 64)
            nc.tensor.transpose(ps[:, 7, 0:N_GAINS], gain_rows, ident[0:N_GAINS, 0:N_GAINS]).then_inc(gains_turned, 1)
            for slab in range(2):
                for u in range(8):
                    if slab == 0:
                        if u in (0, 1, 3):
                            turn(0, (u + 3) // 2)
                        xt_ready(0, 2 * u + 1)
                    token_unit(U_DQKV + 8 * slab + u, xt, 2 * u, 4 + 2 * slab, u == 0, u == 7)
                    if slab == 1 and u == 1:
                        c_turn(0)
            def project_q(g, i=0):
                b = U_ATT + 8 * g
                for u in range(2):
                    weight_unit(b + u, latent_t, 2 * u, 0, u == 0, u == 1, i * 8)

            pe.wait_ge(c_scaled, NT)
            pe.wait_ge(tail_made, 1)
            for t in range(NT):
                for k in range(KT):
                    hi, lo = xt[:, k, t * P:(t + 1) * P], xt[:, k, SEQ + t * P:SEQ + (t + 1) * P]
                    o = ps[:, 4 + t, 0:ROPE]
                    mm(o, hi, tail_hi[:, k, :], start=k == 0, stop=False)
                    mm(o, hi, tail_lo[:, k, :], start=False, stop=False)
                    end = mm(o, lo, tail_hi[:, k, :], start=False, stop=k == KT - 1)
            end.then_inc(tail_done, 1)
            pe.wait_ge(ct_made, LT)
            project_q(0)
            c_turn(1)
            pe.wait_ge(kr_copied, 1)
            for a in range(2):
                for t in range(NT):
                    end = nc.tensor.transpose(ps[:, 4, a * SEQ + t * P:a * SEQ + (t + 1) * P],
                                              k_rope[:, t, a, :, :].rearrange("p r j -> p (r j)"), ident)
            end.then_inc(kr_turned, 1)

            def project_k(g, i=0):
                b = U_ATT + 8 * g + 2
                for u in range(2):
                    weight_unit(b + u, latent_t, LT + 2 * u, 4, u == 0, u == 1, i * 8)

            def project_rope(g, i=0):
                pe.wait_ge(k_summed, g + 1 + i)
                b = U_ATT + 8 * g + 4
                for u in range(2):
                    weight_unit(b + u, latent_t, 2 * u, 4, u == 0, u == 1, i * 8, blocks=2)

            def project_v(g, i=0):
                b = U_ATT + 8 * g + 6
                for u in range(2):
                    token_unit(b + u, latent_t, LT + 2 * u, 6, u == 0, u == 1, i * 8)

            def scores(g, i=0):
                pe.wait_ge(q_made, g + 1 + i)
                pe.wait_ge(k_made, g + 1 + i)
                pe.wait_ge(rotated, g + 2 + i)
                for h in range(GH):
                    if h == 2:
                        pe.wait_ge(v_made, g + 1 + i)
                    for t in range(NT):
                        lo, hi = SCORE_COLS[t]
                        o, keys = ps[:, 4 + h, lo:hi], (t + 1) * P

                        def three(rows, q, k, start, stop):
                            q_hi, q_lo = q[rows, t * P:(t + 1) * P], q[rows, SEQ + t * P:SEQ + (t + 1) * P]
                            k_hi, k_lo = k[rows, 0:keys], k[rows, SEQ:SEQ + keys]
                            mm(o, q_hi, k_hi, start=start, stop=False)
                            mm(o, q_hi, k_lo, start=False, stop=False)
                            return mm(o, q_lo, k_hi, start=False, stop=stop)

                        three(slice(0, P), q_t[:, h, :], k_t[:, h, :], True, False)
                        rows = slice(h * HALF, (h + 1) * HALF)
                        three(rows, qr_t[:, 0, :], kr_t[:, 0, :], False, False)
                        end = three(rows, qr_t[:, 1, :], kr_t[:, 1, :], False, True)
                    if h % 2 == 1:
                        end.then_inc(scores_done, 1)

            def turn_probs(g, i=0):
                pe.wait_ge(probs_made, 8 * (g + 1) + i * 8)
                pe.wait_ge(q_summed, min(g + 2, GROUPS) + i)
                for h in range(GH):
                    for c in (0, P, 2 * P):
                        end = nc.tensor.transpose(ps[:, h, c:c + P], probs[:, h, c:c + P], ident)
                end.then_inc(probs_turned, 1)

            def values(g, i=0):
                pe.wait_ge(pt_made, 2 * (g + 1) + i * 2)
                pe.wait_ge(v_made, g + 1 + i)
                for h in range(GH):
                    c = slice(h * V_HEAD, (h + 1) * V_HEAD)
                    halves = ps[:, h, :].rearrange("p (a n) -> p a n", a=2)
                    mm(ps[:, h, :], v_hi[:, 0, c], p_t[:, h, 0:4 * P], start=True, stop=False)
                    mm(ps[:, h, 0:SEQ], v_lo[:, 0, c], p_t[:, h, 0:2 * P], start=False, stop=False)
                    mm(ps[:, h, P:SEQ], v_lo[:, 1, c], p_t[:, h, 4 * P:5 * P], start=False, stop=False)
                    end = mm(halves[:, :, P:2 * P], v_hi[:, 1, c],
                             p_t[:, h, 4 * P:6 * P].rearrange("p (a n) -> p a n", a=2), start=False, stop=True)
                end.then_inc(o_done, 1)

            def attention_step(g, i=0):
                scores(g, i)
                if g > 0:
                    pe.wait_ge(o_summed, g + i)
                project_q(g + 1, i)
                pe.wait_ge(scores_masked, 8 * (g + 1) + i * 8)
                project_k(g + 1, i)
                turn_probs(g, i)
                project_rope(g + 1, i)
                values(g, i)
                project_v(g + 1, i)

            pe.wait_ge(ct_made, 2 * LT)
            pe.wait_ge(rot_step, 2)
            project_k(0)
            project_rope(0)
            project_v(0)
            attention_step(0)
            with pe.Fori(0, GROUPS - 2) as i:
                attention_step(1, i)
            scores(GROUPS - 1)
            turn_probs(GROUPS - 1)
            values(GROUPS - 1)

            pe.wait_ge(o_made, GROUPS)
            for n in range(SLABS):
                if n >= 2:
                    pe.wait_ge(slab_read, S_WO + n - 1)
                for u in range(8):
                    token_unit(U_WO + 8 * n + u, xt, 2 * u, 4 + 2 * (n % 2), u == 0, u == 7)
                if n >= 1:
                    turn(1, n - 1)

            def mlp(layer, norm_index):
                s0 = layer * FF_SLABS

                def up(b, s, dyn=0, s_dyn=0):
                    if s >= 2:
                        pe.wait_ge(up_summed, s0 + s + s_dyn)
                    for u in range(8):
                        if s == 0:
                            xt_ready(norm_index, max(2 * u + 1, 11))
                        weight_unit(b + u, xt2, 2 * u, 0 if s == 0 else 4, u == 0, u == 7, dyn)
                        if s == 0 and u == 1:
                            turn(norm_index, SLABS - 1)

                def down(b, s, dyn=0, s_dyn=0, closing=False):
                    pe.wait_ge(up_made, s0 + s + 1 + s_dyn)
                    for n in range(SLABS):
                        pe.wait_ge(slab_read, S_MLP[layer] + s * SLABS + n - 1 + s_dyn * SLABS)
                        for u in range(2):
                            token_unit(b + 2 * n + u, mid[:, s % 2, :, :], 2 * u, 2 * (n % 2),
                                       u == 0, u == 1, dyn)
                        if closing and n >= 1:
                            turn(2, n - 1)

                b = U_MLP[layer]
                up(b, 0)
                up(b + 8, 1)
                down(b + 16, 0)
                up(b + 24, 2)
                down(b + 32, 1)
                b += 32
                with pe.Fori(0, FF_SLABS // 2 - 2) as i:
                    up(b + 8, 3, i * 32, i * 2)
                    down(b + 16, 2, i * 32, i * 2)
                    up(b + 24, 4, i * 32, i * 2)
                    down(b + 32, 3, i * 32, i * 2)
                b = U_MLP[layer] + 16 * FF_SLABS - 24
                up(b, FF_SLABS - 1)
                down(b + 8, FF_SLABS - 2)
                down(b + 16, FF_SLABS - 1, closing=layer == 0)

            def pool_products(g):
                xt_ready(2, LT * g + LT - 1)
                if g < 2:
                    pe.wait_ge(slab_read, S_POOL - 1 + g)
                else:
                    pe.wait_ge(pool_copied, g - 1)
                for u in range(2):
                    token_unit(U_POOL + 2 * g + u, xt, LT * g + 2 * u, 2 * (g % 2), u == 0, u == 1)

            def pool_windows(g):
                pe.wait_ge(pool_copied, g + 1)
                if g == 0:
                    pe.wait_ge(bands_scaled, NT)
                    xt_ready(2, KT - 1)
                if g >= 2:
                    pe.wait_ge(slab_read, S_POOL + g - 1)
                o, z = 4 + 2 * (g % 2), pool_sums[g % 2]
                mm(ps[:, o, :], bands[:, g, 0:P], z[:, 0, :], start=True, stop=True)
                mm(ps[:, o + 1, :], bands[:, g, P:2 * P], z[:, 0, :], start=True, stop=False)
                mm(ps[:, o + 1, :], bands[:, g, 2 * P:3 * P], z[:, 1, :], start=False, stop=True).then_inc(pooled, 1)

            mlp(0, 1)
            pool_products(0)
            pool_products(1)
            turn(2, SLABS - 1)
            pool_products(2)
            pool_windows(0)
            pool_products(3)
            pool_windows(1)
            pe.wait_ge(pool_copied, 3)
            turn(3, 0)
            pool_windows(2)
            pe.wait_ge(pool_copied, 4)
            turn(3, 1)
            pool_windows(3)
            turn(3, 2)
            mlp(1, 3)


_INS = ["x", "positions", "ln_mix", "ln_mlp", "w_dqkv", "q_norm", "kv_norm", "w_uq", "w_ukv", "w_o",
        "w_pool", "pool_scale", "w_up", "w_down", "final_norm"]


def shape_constants():
    causal = np.zeros((P, 2 * P), np.float32)
    causal[:, P:] = np.where(np.arange(P)[None, :] <= np.arange(P)[:, None], 0.0, MASKED)
    exponent = np.arange(0, ROPE, 2, dtype=np.float32) / np.float32(ROPE)
    inv_freq = (np.float32(1.0) / np.power(np.float32(ROPE_THETA), exponent)).astype(np.float32)
    first = np.concatenate([np.eye(P, dtype=np.float32), causal, np.tile(inv_freq, P // HALF)[:, None]], axis=1)
    s, t = np.arange(SEQ)[:, None], np.arange(SEQ)[None, :]
    bands = []
    for w in WINDOWS:
        inside = (s <= t) & (s > t - w)
        bands.append((inside / np.minimum(t + 1, w) - (s == t)).astype(np.float32))
    second = np.concatenate([np.concatenate([b[0:P, :], b[P:, P:]], axis=1) for b in bands], axis=1)
    return np.ascontiguousarray(first), np.ascontiguousarray(second)


def kernel(**inputs):
    import concourse.bacc as _bacc
    from concourse.bass_utils import run_bass_kernel_spmd as _run

    nc = _bacc.Bacc("TRN2", target_bir_lowering=False, num_devices=1, dynamic_dma_scratch_size=8192)
    arrays, args = {}, []
    consts, bands = shape_constants()
    given = [(name, np.ascontiguousarray(inputs[name])) for name in _INS]
    for name, a in given + [("shape_consts", consts), ("band_consts", bands)]:
        arrays[f"in_{name}"] = a
        args.append(nc.dram_tensor(f"in_{name}", a.shape, mybir.dt.from_np(a.dtype), kind="ExternalInput").ap())
    args.append(nc.dram_tensor("out_0", (1, SEQ, D_MODEL), F32, kind="ExternalOutput").ap())
    trunk(nc, *args)
    r = _run(nc, [arrays], core_ids=[0])
    return r.results[0]["out_0"]
```

```python
import math
from contextlib import ExitStack

import numpy as np

import concourse.bass as bass
from concourse import mybir

F32 = mybir.dt.float32
F32R = mybir.dt.float32r
I32 = mybir.dt.int32
ALU = mybir.AluOpType
ACT = mybir.ActivationFunctionType

P = 128
D_MODEL = 2048
SEQ = 256
NT = SEQ // P
KT = D_MODEL // P
N_HEADS = 16
LORA = 512
LT = LORA // P
NOPE = 128
ROPE = 64
HALF = ROPE // 2
QK_HEAD = NOPE + ROPE
V_HEAD = 128
GH = 4
GROUPS = N_HEADS // GH
ROPE_THETA = 10000.0
WINDOWS = (2, 4, 8, 16)
D_FF = 4 * D_MODEL
EPS = 1e-6
SCALE = 1.0 / math.sqrt(QK_HEAD)
MASKED = -3.0e38

COLS = 512
LAST_COLS = slice(D_MODEL - COLS, D_MODEL)
RAW_SLOTS = 4
LEAD = 4
SLABS = D_MODEL // COLS
FF_SLABS = D_FF // COLS
FB = COLS // P

U_DQKV = 0
U_ATT = U_DQKV + 2 * KT // 2
U_WO = U_ATT + 8 * GROUPS
U_MLP = (U_WO + SLABS * KT // 2, 0)
U_POOL = U_MLP[0] + 16 * FF_SLABS
U_MLP = (U_MLP[0], U_POOL + 2 * SLABS)
U_END = U_MLP[1] + 16 * FF_SLABS

TURN_BANK = ((0, 2, 0, 6), (0, 2, 4, 6), (4, 6, 4, 6), (0, 2, 4, 6))
S_WO = 0
S_MLP = (SLABS, SLABS + FF_SLABS * SLABS + SLABS)
S_POOL = S_MLP[0] + FF_SLABS * SLABS

S_END = S_MLP[1] + FF_SLABS * SLABS
ADDED_BEFORE = (0, S_WO, S_MLP[0] + (FF_SLABS - 1) * SLABS, S_POOL,
                S_MLP[1] + (FF_SLABS - 1) * SLABS)
SCORE_COLS = ((0, P), (P, 3 * P))

GAIN_COL = (0, 2 * KT, KT, 3 * KT)
Q_GAIN = 4 * KT
N_GAINS = 4 * KT + 2 * LT

TWO_PI_A = 6.28125
TWO_PI_B = float(np.float32(2 * math.pi - TWO_PI_A))
TWO_PI_B = float(np.float32(np.round(TWO_PI_B * 2**20) / 2**20))
TWO_PI_C = float(np.float32(2 * math.pi - TWO_PI_A - TWO_PI_B))
PI_IN = 3.1415925
ROUNDER = 1.5 * 2.0**23


def trunk(nc, x, positions, ln_mix, ln_mlp, w_dqkv, q_norm, kv_norm, w_uq, w_ukv, w_o,
          w_pool, pool_scale, w_up, w_down, final_norm, shape_consts, band_consts, out):
    ctx = ExitStack()
    with ctx:
        def sb(name, shape, dt=F32):
            return ctx.enter_context(nc.sbuf_tensor(name, shape, dt))

        def sem(name):
            return ctx.enter_context(nc.semaphore(name))

        resid = sb("resid", [P, NT, D_MODEL])
        weight_raw = sb("weight_raw", [P, RAW_SLOTS, 4, COLS])
        weight_hi = sb("weight_hi", [P, LEAD, 2, COLS], F32R)
        weight_lo = sb("weight_lo", [P, LEAD, 2, COLS], F32R)
        xt = sb("xt", [P, KT, 2 * SEQ], F32R)
        xt2 = sb("xt2", [P, KT, 2 * SEQ], F32R)
        mid = sb("mid", [P, 2, FB, 2 * SEQ], F32R)
        scratch = sb("scratch", [P, 2 * D_MODEL])
        row_gain = sb("row_gain", [P, D_MODEL])
        early = sb("early", [P, 1536])
        p_t = sb("p_t", [P, GH, 6 * P], F32R)
        cos_t = sb("cos_t", [P, 2, SEQ])
        sin_t = sb("sin_t", [P, 2, SEQ])
        consts = sb("consts", [P, 3 * P + 1])
        gain_col = sb("gain_col", [P, N_GAINS])
        small = sb("small", [P, 96])
        ps = ctx.enter_context(nc.psum_tensor("ps", [P, 8, COLS], F32))

        ident = consts[:, 0:P]
        causal = consts[:, P:3 * P]
        inv_freq = consts[:, 3 * P:3 * P + 1]
        latent_t = mid[:, :, :, :].rearrange("p a b c -> p (a b) c")
        q_t = xt2[:, 0:4, :]
        k_t = xt2[:, 4:8, :]
        v_hi = xt2[:, 8:10, :]
        v_lo = xt2[:, 10:12, :]
        qr_t = xt2[:, 12:14, :]
        kr_t = xt2[:, 14:16, :]
        turned_into = (xt, xt2, xt, xt2)
        latent = scratch[:, 0:2 * NT * LORA].rearrange("p (t n) -> p t n", t=NT)
        tail_raw = early[:, 0:KT * ROPE].rearrange("p (k c) -> p k c", k=KT)
        tail_hi = q_t[:, 0:2, :].rearrange("p a (k c) -> p (a k) c", c=ROPE)
        tail_lo = q_t[:, 2:4, :].rearrange("p a (k c) -> p (a k) c", c=ROPE)
        k_rope = early[:, KT * ROPE:KT * ROPE + 512].rearrange("p (t a r j) -> p t a r j", t=NT, a=2, r=4)
        pos_i = early[:, 8 * P:8 * P + SEQ].bitcast(I32)
        gain_rows = early[0:N_GAINS, 11 * P:12 * P]
        probs = early[:, :].rearrange("p (h c) -> p h c", h=GH)
        bands = early[:, :].rearrange("p (g c) -> p g c", g=SLABS)
        fold_b = [scratch[:, s * 1024:(s + 1) * 1024].rearrange("p (b n) -> p b n", b=FB) for s in (0, 1)]
        fold_s = [scratch[:, s * 1024:(s + 1) * 1024].rearrange("p (b n) -> p b n", b=FB) for s in (2, 3)]
        rot_b = scratch[:, 1024:1536].rearrange("p (a n) -> p a n", a=2)
        rot_x = scratch[:, 1536:2048].rearrange("p (a n) -> p a n", a=2)
        rot_c = scratch[:, 3072:3584].rearrange("p (a n) -> p a n", a=2)
        rot_s = scratch[:, 3584:4096].rearrange("p (a n) -> p a n", a=2)
        kr_low = rot_c[0:ROPE, 0, :]
        kr_sum = rot_s[0:ROPE, 0, :]
        last_gained = early[:, 0:NT * COLS].rearrange("p (t n) -> p t n", t=NT)
        squares_out = scratch[:, 1024:2048].rearrange("p (t n) -> p t n", t=NT)
        pool_sums = [scratch[:, s * 1024:(s + 1) * 1024].rearrange("p (t n) -> p t n", t=NT) for s in (2, 3)]
        result = scratch[:, :].rearrange("p (t n) -> p t n", t=NT)
        sumsq = small[:, 0:8].rearrange("p (t s) -> p t s", t=NT)
        total = small[:, 8:10]
        root = small[:, 10:12]
        rstd = small[:, 12:14]
        rstd_sq = small[:, 14:16]
        eps = small[:, 16:17]
        c_sumsq = small[:, 20:24].rearrange("p (j t) -> p j t", j=2)
        c_root = small[:, 24:28].rearrange("p (j t) -> p j t", j=2)
        c_rstd = small[:, 28:32].rearrange("p (j t) -> p j t", j=2)
        c_scale = small[:, 32:36].rearrange("p (j t) -> p j t", j=2)
        row_max = small[:, 40:48]
        neg_max = small[:, 48:56]
        row_sum = small[:, 56:64]
        inv_sum = small[:, 64:72]
        step_mark = small[:, 72:74]

        x_in = [sem(f"x_in{s}") for s in range(SLABS)]
        consts_in, gains_in, pos_in, tail_in = sem("consts_in"), sem("gains_in"), sem("pos_in"), sem("tail_in")
        band_in, scale_in, final_in, out_done = sem("band_in"), sem("scale_in"), sem("final_in"), sem("out_done")
        raw_in = [sem(f"raw_in{s}") for s in range(RAW_SLOTS)]
        unit0_in = sem("unit0_in")
        hi_made, lo_made, unit_used = sem("hi_made"), sem("lo_made"), sem("unit_used")
        gains_turned, gains_ready, eps_set = sem("gains_turned"), sem("gains_ready"), sem("eps_set")
        squared, totalled, rooted, rstd_made = sem("squared"), sem("totalled"), sem("rooted"), sem("rstd_made")
        mean_made, rstd_sq_made = sem("mean_made"), sem("rstd_sq_made")
        turned, xt_hi_made, xt_made = sem("turned"), sem("xt_hi_made"), sem("xt_made")
        slab_read, bands_scaled = sem("slab_read"), sem("bands_scaled")
        pooled, pool_scaled = sem("pooled"), sem("pool_scaled")
        up_low, up_summed = sem("up_low"), sem("up_summed")
        up_squared, up_hi, up_made = sem("up_squared"), sem("up_hi"), sem("up_made")
        tail_hi_made, tail_made = sem("tail_hi_made"), sem("tail_made")
        tail_done, c_squared, c_rooted, c_rstd_made = sem("tail_done"), sem("c_squared"), sem("c_rooted"), sem("c_rstd_made")
        c_scale_made = sem("c_scale_made")
        c_scaled, c_turned, ct_hi_made, ct_made = sem("c_scaled"), sem("c_turned"), sem("ct_hi_made"), sem("ct_made")
        kr_low_made, kr_summed, kr_back = sem("kr_low_made"), sem("kr_summed"), sem("kr_back")
        kr_copied, kr_turned = sem("kr_copied"), sem("kr_turned")
        table_step, angles_made, tables_made = sem("table_step"), sem("angles_made"), sem("tables_made")
        rot_low, rot_step, rot_made, rot_hi, rotated = (sem("rot_low"), sem("rot_step"), sem("rot_made"),
                                                        sem("rot_hi"), sem("rotated"))
        r_summed = sem("r_summed")
        q_low, q_summed, q_hi, q_made = sem("q_low"), sem("q_summed"), sem("q_hi"), sem("q_made")
        k_low, k_summed, k_hi, k_made = sem("k_low"), sem("k_summed"), sem("k_hi"), sem("k_made")
        v_hi_made, v_made = sem("v_hi_made"), sem("v_made")
        scores_done, scores_masked, neg_max_made = sem("scores_done"), sem("scores_masked"), sem("neg_max_made")
        exp_made, inv_made, probs_made = sem("exp_made"), sem("inv_made"), sem("probs_made")
        probs_turned, pt_hi_made, pt_made = sem("probs_turned"), sem("pt_hi_made"), sem("pt_made")
        o_done, o_low, o_summed, o_hi, o_made = (sem("o_done"), sem("o_low"), sem("o_summed"),
                                                 sem("o_hi"), sem("o_made"))
        last_added = sem("last_added")
        gained, final_t0, final_t1 = sem("gained"), sem("final_t0"), sem("final_t1")

        block = ctx.enter_context(nc.Block())

        @block.sync
        def _(sp):
            def load(c, source, dyn=0, width=COLS):
                if c >= RAW_SLOTS:
                    sp.wait_ge(lo_made, 2 * (c - RAW_SLOTS) + 2 + dyn)
                sp.dma_start(weight_raw[:, c % RAW_SLOTS, :, 0:width], source).then_inc(raw_in[c % RAW_SLOTS], 16)

            def rows(w, first, n=4):
                return w[first:first + n * P, :].rearrange("(k p) n -> p k n", p=P)

            def load_x(s):
                cols = slice(s * COLS, (s + 1) * COLS)
                sp.dma_start(resid[:, :, cols], x[0].rearrange("(t p) n -> p t n", p=P)[:, :, cols]
                             ).then_inc(x_in[s], 16)

            sp.dma_start(consts[:, :], shape_consts).then_inc(consts_in, 16)
            for slab in range(2):
                for c in range(4):
                    if slab == 0 and c != 1:
                        load_x(c)
                    if slab == 0 and c == 0:
                        first = 0
                        for g in (ln_mix, ln_mlp, q_norm, kv_norm):
                            n = g.shape[0] * g.shape[1] // P
                            sp.dma_start(gain_rows[first:first + n, :],
                                         g.rearrange("l (k p) -> (l k) p", p=P)).then_inc(gains_in, 16)
                            first += n
                    chunk = rows(w_dqkv[0], 4 * P * c)[:, :, slab * COLS:(slab + 1) * COLS]
                    if slab == 0 and c == 0:
                        sp.dma_start(weight_raw[:, 0, 0:2, :], chunk[:, 0:2, :]).then_inc(unit0_in, 16)
                        load_x(1)
                        sp.dma_start(weight_raw[:, 0, 2:4, :], chunk[:, 2:4, :]).then_inc(raw_in[0], 16)
                    else:
                        load(U_DQKV // 2 + 4 * slab + c, chunk)
            sp.dma_start(tail_raw, w_dqkv[0, :, 2 * LORA:2 * LORA + ROPE]
                         .rearrange("(k p) n -> p k n", p=P)).then_inc(tail_in, 16)
            uq = rows(w_uq[0], 0).rearrange("p k (h c) -> p k h c", h=N_HEADS)
            ukv = rows(w_ukv[0], 0).rearrange("p k (h c) -> p k h c", h=N_HEADS)

            def load_heads(c, w, h0, c0, width, dyn, h_dyn):
                if c >= RAW_SLOTS:
                    sp.wait_ge(lo_made, 2 * (c - RAW_SLOTS) + 2 + dyn)
                for k in range(LT):
                    dst = weight_raw[:, c % RAW_SLOTS, k, 0:GH * width].rearrange("p (h c) -> p h c", h=GH)
                    sp.dma_start(dst, w[:, k, bass.ds(h_dyn + h0, GH), c0:c0 + width]).then_inc(
                        raw_in[c % RAW_SLOTS], 16)

            def load_group(c, dyn, h_dyn):
                load_heads(c, uq, 0, 0, NOPE, dyn, h_dyn)
                load_heads(c + 1, ukv, 0, 0, NOPE, dyn, h_dyn)
                load_heads(c + 2, uq, 0, NOPE, ROPE, dyn, h_dyn)
                load_heads(c + 3, ukv, 0, NOPE, V_HEAD, dyn, h_dyn)

            with sp.Fori(0, GROUPS) as g:
                load_group(U_ATT // 2, g * 8, g * GH)
            for slab in range(SLABS):
                for c in range(4):
                    load(U_WO // 2 + 4 * slab + c, rows(w_o[0], 4 * P * c)[:, :, slab * COLS:(slab + 1) * COLS])

            def load_up(layer, c, s, dyn=0):
                for j in range(4):
                    load(c + j, w_up[layer, 4 * P * j:4 * P * (j + 1), bass.ds(s * COLS, COLS)]
                         .rearrange("(k p) n -> p k n", p=P), dyn)

            def load_down(layer, c, s, dyn=0):
                for n in range(SLABS):
                    load(c + n, w_down[layer, bass.ds(s * COLS, COLS), n * COLS:(n + 1) * COLS]
                         .rearrange("(k p) n -> p k n", p=P), dyn)

            def load_mlp(layer):
                c = U_MLP[layer] // 2
                load_up(layer, c, 0)
                with sp.Fori(0, FF_SLABS // 2 - 1) as i:
                    load_up(layer, c + 4, i * 2 + 1, i * 32)
                    load_down(layer, c + 8, i * 2, i * 32)
                    load_up(layer, c + 12, i * 2 + 2, i * 32)
                    load_down(layer, c + 16, i * 2 + 1, i * 32)
                last = c + 4 + 16 * (FF_SLABS // 2 - 1)
                load_up(layer, last, FF_SLABS - 1)
                load_down(layer, last + 4, FF_SLABS - 2)
                load_down(layer, last + 8, FF_SLABS - 1)

            load_mlp(0)
            for g in range(SLABS):
                load(U_POOL // 2 + g, rows(w_pool[0, g], 0))
            load_mlp(1)
            for s in range(SLABS):
                cols = slice(s * COLS, (s + 1) * COLS)
                for t, made in ((1, final_t1), (0, final_t0)):
                    sp.wait_ge(made, s + 1)
                    sp.dma_start(out[0, t * P:(t + 1) * P, cols], result[:, t, cols]).then_inc(out_done, 16)
            sp.wait_ge(out_done, 16 * SLABS * NT)

        @block.gpsimd
        def _(pool):
            pool.dma_start(pos_i, positions.to_broadcast([P, SEQ])).then_inc(pos_in, 16)
            pool.dma_start(row_gain[:, :], pool_scale.to_broadcast([P, D_MODEL])).then_inc(scale_in, 16)
            pool.wait_ge(probs_turned, GROUPS)
            pool.dma_start(early[:, :], band_consts).then_inc(band_in, 16)
            pool.wait_ge(slab_read, S_POOL + SLABS)
            pool.dma_start(row_gain[:, :], final_norm.rearrange("(a n) -> a n", a=1)
                           .to_broadcast([P, D_MODEL])).then_inc(final_in, 16)
            pool.wait_ge(final_in, 16)
            for s in range(SLABS - 1):
                pool.wait_ge(squared, NT * (4 * SLABS + s + 1))
                for t in range(NT):
                    cols = resid[:, t, s * COLS:(s + 1) * COLS]
                    nc.gpsimd.tensor_tensor(cols, cols, row_gain[:, s * COLS:(s + 1) * COLS],
                                            ALU.mult).then_inc(gained, 1)

        def gained_slab(s, t):
            return last_gained[:, t, :] if s == SLABS - 1 else resid[:, t, s * COLS:(s + 1) * COLS]

        def raw_of(v):
            return weight_raw[:, (v // 2) % RAW_SLOTS, 2 * (v % 2):2 * (v % 2) + 2, :]

        def raw_ready(v):
            c = v // 2
            per = lambda j: 16 * LT if U_ATT // 2 <= j < U_WO // 2 else 16
            return sum(per(j) for j in range(c % RAW_SLOTS, c + 1, RAW_SLOTS))

        def rope_views(dst, v, raw):
            for a in range(2):
                yield (dst[:, v % LEAD, :, a * P:(a + 1) * P].rearrange("p k (h j) -> p k h j", h=GH),
                       raw[:, :, 0:GH * ROPE].rearrange("p k (h a j) -> p k a h j", h=GH, a=2)[:, :, a])

        def is_rope(v):
            return U_ATT <= v < U_WO and (v - U_ATT) % 8 in (4, 5)

        @block.scalar
        def _(act):
            def split(v, dyn=0, raw_dyn=0):
                if v >= U_END:
                    return
                if v == 0:
                    act.wait_ge(unit0_in, 16)
                else:
                    act.wait_ge(raw_in[(v // 2) % RAW_SLOTS], raw_ready(v) + raw_dyn)
                if v >= LEAD:
                    act.wait_ge(unit_used, v - LEAD + 1 + dyn)
                if is_rope(v):
                    for dst, src in rope_views(weight_hi, v, raw_of(v)):
                        last = nc.scalar.copy(dst, src)
                else:
                    last = nc.scalar.copy(weight_hi[:, v % LEAD, :, :], raw_of(v))
                last.then_inc(hi_made, 1)

            def position(k, dyn=0, raw_dyn=0):
                split(k + LEAD, dyn, raw_dyn)

            def squares(n, s):
                if n == 0:
                    act.wait_ge(x_in[s], 16)
                else:
                    act.wait_ge(slab_read, ADDED_BEFORE[n] + s + 1)
                if n + s > 0:
                    act.wait_ge(squared, NT * (SLABS * n + s))
                if n > 0 and s == 0:
                    act.wait_ge(totalled, n)
                for t in range(NT):
                    nc.scalar.activation(squares_out[:, t, :], resid[:, t, s * COLS:(s + 1) * COLS], ACT.Square,
                                         accum_out=sumsq[:, t, s:s + 1]).then_inc(squared, 1)

            def root_of_mean(i, n):
                act.wait_ge(totalled, n + 1)
                nc.scalar.activation(root, total, ACT.Sqrt, bias=eps, scale=1.0 / D_MODEL).then_inc(rooted, 1)

            def turn_hi(n, s):
                for k in range(4 * s, 4 * s + 4):
                    act.wait_ge(turned, 8 * n + k // 2 + 1)
                    bank = TURN_BANK[n][s] + k // 2 % 2
                    g = GAIN_COL[n] + k
                    nc.scalar.activation(turned_into[n][:, k, 0:SEQ], ps[:, bank, (k % 2) * SEQ:(k % 2 + 1) * SEQ],
                                         ACT.Copy, scale=gain_col[:, g:g + 1]).then_inc(xt_hi_made, 1)

            def c_norm_start(j):
                act.wait_ge(unit_used, U_DQKV + 8 * (j + 1))
                for t in range(NT):
                    nc.scalar.activation(latent[:, t, j * LORA:(j + 1) * LORA], ps[:, 4 + 2 * j + t, :], ACT.Square,
                                         scale=rstd[:, t:t + 1], accum_out=c_sumsq[:, j, t:t + 1]).then_inc(c_squared, 1)
                act.wait_ge(c_squared, 2 * j + 2)
                nc.scalar.activation(c_root[:, j, :], c_sumsq[:, j, :], ACT.Sqrt, bias=eps,
                                     scale=1.0 / LORA).then_inc(c_rooted, 1)
                act.wait_ge(c_scale_made, j + 1)
                for t in range(NT):
                    nc.scalar.activation(latent[:, t, j * LORA:(j + 1) * LORA], ps[:, 4 + 2 * j + t, :], ACT.Copy,
                                         scale=c_scale[:, j, t:t + 1]).then_inc(c_scaled, 1)

            def c_round(j):
                for k in range(LT):
                    act.wait_ge(c_turned, 2 * j + k // 2 + 1)
                    g = Q_GAIN + j * LT + k
                    nc.scalar.activation(latent_t[:, j * LT + k, 0:SEQ],
                                         ps[:, 6 * j + k // 2, (k % 2) * SEQ:(k % 2 + 1) * SEQ], ACT.Copy,
                                         scale=gain_col[:, g:g + 1]).then_inc(ct_hi_made, 1)

            def fold_low(k, dyn, low, side):
                act.wait_ge(unit_used, k + 1 + dyn)
                nc.scalar.copy(fold_b[side], ps[:, 4 * side:4 * side + 4, SEQ:2 * SEQ]).then_inc(low, 1)

            def round_hi(n, dyn, value_made, dst, value, hi):
                act.wait_ge(value_made, n + 1 + dyn)
                nc.scalar.copy(dst, value).then_inc(hi, 1)

            act.wait_ge(gains_turned, 1)
            nc.scalar.copy(gain_col[:, :], ps[:, 7, 0:N_GAINS]).then_inc(gains_ready, 1)
            act.wait_ge(gains_ready, 1)
            for s in range(SLABS):
                turn_hi(0, s)
                split(2 * s)
                split(2 * s + 1)
                if s == 0:
                    act.wait_ge(angles_made, 1)
                    for a in range(2):
                        nc.scalar.activation(sin_t[:, a, :], rot_c[:, 0, :], ACT.Sin).then_inc(tables_made, 1)
                        nc.scalar.activation(cos_t[:, a, :], rot_c[:, 1, :], ACT.Sin).then_inc(tables_made, 1)
                squares(0, s)
            act.wait_ge(eps_set, 1)
            root_of_mean(0, 0)
            for k in range(U_DQKV + 4, U_ATT):
                if k == U_ATT - 1:
                    c_norm_start(1)
                position(k)
                if k == 7:
                    act.wait_ge(rstd_made, 1)
                    c_norm_start(0)
                if k == 8:
                    act.wait_ge(tail_in, 16)
                    nc.scalar.copy(tail_hi, tail_raw).then_inc(tail_hi_made, 1)
                if k == 10:
                    act.wait_ge(tail_done, 1)
                    nc.scalar.copy(kr_low, ps[0:ROPE, 2, SEQ:2 * SEQ]).then_inc(kr_low_made, 1)
                if k == 11:
                    c_round(0)
                if k == 12:
                    act.wait_ge(kr_back, 1)
                    for t in range(NT):
                        for r in range(4):
                            last = nc.scalar.activation(
                                k_rope[:, t, :, r, :],
                                ps[:, 3, t * ROPE:(t + 1) * ROPE].rearrange("p (a j) -> p a j", a=2),
                                ACT.Copy, scale=rstd[:, t:t + 1])
                    last.then_inc(kr_copied, 1)
            c_round(1)
            round_hi(0, 0, rot_made, kr_t[:, :, 0:SEQ], rot_x, rot_hi)

            def q_low_part(g, dyn=0):
                fold_low(U_ATT + 8 * g + 1, dyn * 8, q_low, 0)

            def q_round(g, dyn=0):
                round_hi(g, dyn, q_summed, q_t[:, :, 0:SEQ], fold_s[0], q_hi)

            def k_low_part(g, dyn=0):
                act.wait_ge(unit_used, U_ATT + 8 * g + 4 + dyn * 8)
                for half in (slice(0, 2), slice(2, 4)):
                    nc.scalar.copy(fold_b[1][:, half, :], ps[:, 4 + half.start:4 + half.stop, SEQ:2 * SEQ]
                                   ).then_inc(k_low, 1)

            def k_round(g, dyn=0):
                act.wait_ge(k_summed, 2 * g + 2 + 2 * dyn)
                nc.scalar.copy(k_t[:, :, 0:SEQ], fold_s[1]).then_inc(k_hi, 1)

            def r_low_part(g, dyn=0):
                act.wait_ge(unit_used, U_ATT + 8 * g + 6 + dyn * 8)
                bank = 0 if g == 0 else 4
                nc.scalar.copy(rot_b, ps[:, bank:bank + 2, SEQ:2 * SEQ]).then_inc(rot_low, 1)

            def r_round(g, dyn=0):
                round_hi(g + 1, dyn, rot_made, qr_t[:, :, 0:SEQ], rot_x, rot_hi)

            def v_round(g, dyn=0):
                act.wait_ge(unit_used, U_ATT + 8 * g + 8 + dyn * 8)
                nc.scalar.copy(v_hi[:, :, :], ps[:, 6:8, :]).then_inc(v_hi_made, 1)

            def exps(g, dyn=0):
                act.wait_ge(neg_max_made, g + 1 + dyn)
                for h in range(GH):
                    for t in range(NT):
                        i = NT * h + t
                        part = probs[:, h, SCORE_COLS[t][0]:SCORE_COLS[t][1]]
                        nc.scalar.activation(part, part, ACT.Exp, bias=neg_max[:, i:i + 1], scale=SCALE,
                                             accum_out=row_sum[:, i:i + 1]).then_inc(exp_made, 1)

            def pt_round(g, dyn=0):
                act.wait_ge(probs_turned, g + 1 + dyn)
                nc.scalar.copy(p_t[:, :, 0:2 * P], ps[:, 0:4, 0:2 * P]).then_inc(pt_hi_made, 1)
                nc.scalar.copy(p_t[:, :, 4 * P:5 * P], ps[:, 0:4, 2 * P:3 * P]).then_inc(pt_hi_made, 1)

            def o_low_part(g, dyn=0):
                act.wait_ge(o_done, g + 1 + dyn)
                nc.scalar.copy(fold_b[0], ps[:, 0:4, SEQ:2 * SEQ]).then_inc(o_low, 1)

            def o_round(g, dyn=0):
                act.wait_ge(o_summed, g + 1 + dyn)
                nc.scalar.copy(xt[:, bass.ds(dyn * GH + g * GH, GH), 0:SEQ], fold_s[0]).then_inc(o_hi, 1)

            def attention_step(g, i=0):
                b, dyn, raw_dyn = U_ATT + 8 * (g + 1), i * 8, i * 16 * LT
                if g >= 0:
                    exps(g, i)
                position(b, dyn, raw_dyn)
                q_low_part(g + 1, i)
                position(b + 1, dyn, raw_dyn)
                q_round(g + 1, i)
                position(b + 2, dyn, raw_dyn)
                k_low_part(g + 1, i)
                if g >= 0:
                    pt_round(g, i)
                k_round(g + 1, i)
                if g < 0:
                    r_low_part(0)
                position(b + 3, dyn, raw_dyn)
                if g >= 0:
                    r_low_part(g + 1, i)
                    position(b + 4, dyn, raw_dyn)
                    o_low_part(g, i)
                    position(b + 5, dyn, raw_dyn)
                    r_round(g + 1, i)
                else:
                    r_round(0)
                    position(b + 4)
                    position(b + 5)
                position(b + 6, dyn, raw_dyn)
                v_round(g + 1, i)
                if g >= 0:
                    o_round(g, i)
                position(b + 7, dyn, raw_dyn)

            attention_step(-1)
            with act.Fori(0, GROUPS - 2) as i:
                attention_step(0, i)
            attention_step(GROUPS - 2)
            exps(GROUPS - 1)
            for k in range(U_WO, U_WO + 3):
                position(k)
            pt_round(GROUPS - 1)
            position(U_WO + 3)
            o_low_part(GROUPS - 1)
            o_round(GROUPS - 1)

            for k in range(U_WO + 4, U_MLP[0]):
                position(k)
                if (k - U_WO) % 8 == 3 and k - U_WO > 7:
                    turn_hi(1, (k - U_WO) // 8 - 1)
                    squares(1, (k - U_WO) // 8 - 1)

            def mlp(layer, norm_index):
                s0 = layer * FF_SLABS

                def up(b, s, dyn=0, raw_dyn=0):
                    side = 0 if s == 0 else 1
                    for k in range(8):
                        position(b + k, dyn, raw_dyn)
                        if s == 0 and k == 1:
                            turn_hi(norm_index, SLABS - 1)
                            squares(norm_index, SLABS - 1)
                    act.wait_ge(unit_used, b + 8 + dyn)
                    nc.scalar.copy(fold_b[0], ps[:, 4 * side:4 * side + 4, SEQ:2 * SEQ]).then_inc(up_low, 1)

                def square_hi(s, s_dyn=0):
                    round_hi(s0 + s, s_dyn, up_squared, mid[:, s % 2, :, 0:SEQ], fold_s[1], up_hi)

                def down(b, s_up, dyn=0, raw_dyn=0, s_dyn=0):
                    for k in range(8):
                        position(b + k, dyn, raw_dyn)
                        if s_up is not None and k == 1:
                            square_hi(s_up, s_dyn)
                        if s_up is None and k % 2 == 1 and k > 1:
                            squares(norm_index + 1, k // 2 - 1)
                            if layer == 0:
                                turn_hi(norm_index + 1, k // 2 - 1)

                b = U_MLP[layer]
                up(b, 0)
                square_hi(0)
                with act.Fori(0, FF_SLABS // 2 - 1) as i:
                    up(b + 8, 1, i * 32, i * 64)
                    down(b + 16, 1, i * 32, i * 64, i * 2)
                    up(b + 24, 2, i * 32, i * 64)
                    down(b + 32, 2, i * 32, i * 64, i * 2)
                b = U_MLP[layer] + 16 * FF_SLABS - 24
                up(b, FF_SLABS - 1)
                down(b + 8, FF_SLABS - 1)
                down(b + 16, None)

            mlp(0, 1)
            squares(2, SLABS - 1)
            root_of_mean(1, 2)
            for k in range(U_POOL, U_MLP[1]):
                position(k)
                if k == U_POOL + 1:
                    turn_hi(2, SLABS - 1)
            for s in range(SLABS - 1):
                turn_hi(3, s)
                squares(3, s)
            mlp(1, 3)
            act.wait_ge(squared, NT * (5 * SLABS - 1))
            for t in range(NT):
                act.wait_ge(last_added, t + 1)
                nc.scalar.activation(squares_out[:, t, :], resid[:, t, LAST_COLS], ACT.Square,
                                     accum_out=sumsq[:, t, SLABS - 1:SLABS]).then_inc(squared, 1)
            root_of_mean(2, 4)
            act.wait_ge(rstd_made, 3)
            act.wait_ge(gained, NT * SLABS)
            for s in range(SLABS):
                nc.scalar.activation(result[:, 0, s * COLS:(s + 1) * COLS], gained_slab(s, 0), ACT.Copy,
                                     scale=rstd[:, 0:1]).then_inc(final_t0, 1)

        @block.vector
        def _(dve):
            def as_f32(a):
                return a.bitcast(F32)

            def split(v, dyn=0):
                if v >= U_END:
                    return
                dve.wait_ge(hi_made, v + 1 + dyn)
                if is_rope(v):
                    for (dst, src), (hi, _) in zip(rope_views(weight_lo, v, raw_of(v)),
                                                   rope_views(weight_hi, v, raw_of(v))):
                        last = nc.vector.tensor_tensor(dst, src, as_f32(hi), ALU.subtract)
                else:
                    last = nc.vector.tensor_tensor(weight_lo[:, v % LEAD, :, :], raw_of(v),
                                                   as_f32(weight_hi[:, v % LEAD, :, :]), ALU.subtract)
                last.then_inc(lo_made, 1)

            def position(k, dyn=0):
                split(k + LEAD, dyn)

            def mean_square(n):
                dve.wait_ge(squared, NT * SLABS * (n + 1))
                nc.vector.reduce_sum(total, sumsq, mybir.AxisListType.X).then_inc(totalled, 1)

            def make_rstd(i, n):
                mean_square(n)
                dve.wait_ge(rooted, i + 1)
                nc.vector.reciprocal(rstd, root).then_inc(rstd_made, 1)

            def make_rstd_sq(i, n):
                mean_square(n)
                dve.wait_ge(totalled, n + 1)
                nc.vector.tensor_scalar(rstd_sq, total, 1.0 / D_MODEL, EPS, ALU.mult, ALU.add).then_inc(mean_made, 1)
                dve.wait_ge(mean_made, i + 1)
                nc.vector.reciprocal(rstd_sq, rstd_sq).then_inc(rstd_sq_made, 1)
                dve.wait_ge(rstd_sq_made, i + 1)

            def turn_lo(n, s):
                for k in range(4 * s, 4 * s + 4):
                    dve.wait_ge(xt_hi_made, KT * n + k // 2 * 2 + 2)
                    bank = TURN_BANK[n][s] + k // 2 % 2
                    g = GAIN_COL[n] + k
                    nc.vector.scalar_tensor_tensor(
                        out=turned_into[n][:, k, SEQ:2 * SEQ], in0=ps[:, bank, (k % 2) * SEQ:(k % 2 + 1) * SEQ],
                        scalar=gain_col[:, g:g + 1], in1=as_f32(turned_into[n][:, k, 0:SEQ]),
                        op0=ALU.mult, op1=ALU.subtract).then_inc(xt_made, 1)

            def c_norm_factor(j):
                dve.wait_ge(c_rooted, j + 1)
                nc.vector.reciprocal(c_rstd[:, j, :], c_root[:, j, :]).then_inc(c_rstd_made, 1)
                dve.wait_ge(c_rstd_made, j + 1)
                nc.vector.tensor_tensor(c_scale[:, j, :], c_rstd[:, j, :], rstd, ALU.mult).then_inc(c_scale_made, 1)

            def c_low(j):
                for k in range(LT):
                    dve.wait_ge(ct_hi_made, LT * j + k // 2 * 2 + 2)
                    g = Q_GAIN + j * LT + k
                    nc.vector.scalar_tensor_tensor(
                        out=latent_t[:, j * LT + k, SEQ:2 * SEQ],
                        in0=ps[:, 6 * j + k // 2, (k % 2) * SEQ:(k % 2 + 1) * SEQ],
                        scalar=gain_col[:, g:g + 1], in1=as_f32(latent_t[:, j * LT + k, 0:SEQ]),
                        op0=ALU.mult, op1=ALU.subtract).then_inc(ct_made, 1)

            def rope_angles():
                steps = [0]

                def then_wait(instruction):
                    steps[0] += 1
                    instruction.then_inc(table_step, 1)
                    dve.wait_ge(table_step, steps[0])

                angle, turns, r = rot_s[:, 0, :], rot_s[:, 1, :], rot_c[:, 0, :]
                shifted, wrap = rot_c[:, 1, :], rot_s[:, 0, :]
                dve.wait_ge(pos_in, 16)
                dve.wait_ge(consts_in, 16)
                then_wait(nc.vector.tensor_copy(turns, pos_i))
                then_wait(nc.vector.tensor_scalar(angle, turns, inv_freq, None, ALU.mult))
                then_wait(nc.vector.tensor_scalar(turns, angle, 0.5 / math.pi, ROUNDER, ALU.mult, ALU.add))
                then_wait(nc.vector.tensor_scalar(turns, turns, ROUNDER, None, ALU.subtract))
                then_wait(nc.vector.scalar_tensor_tensor(out=r, in0=turns, scalar=-TWO_PI_A, in1=angle,
                                                         op0=ALU.mult, op1=ALU.add))
                for part in (TWO_PI_B, TWO_PI_C):
                    then_wait(nc.vector.scalar_tensor_tensor(out=r, in0=turns, scalar=-part, in1=r,
                                                             op0=ALU.mult, op1=ALU.add))
                then_wait(nc.vector.tensor_scalar(shifted, r, 0.5 * math.pi, None, ALU.add))
                then_wait(nc.vector.tensor_scalar(wrap, shifted, math.pi, -2.0 * math.pi, ALU.is_gt, ALU.mult))
                then_wait(nc.vector.tensor_tensor(shifted, shifted, wrap, ALU.add))
                nc.vector.tensor_scalar(rot_c, rot_c, PI_IN, -PI_IN, ALU.min, ALU.max).then_inc(angles_made, 1)

            def rotate_start(n, source, dyn=0):
                if n >= 1:
                    dve.wait_ge(rot_made, n + dyn)
                    dve.wait_ge(k_made, n + dyn)
                if n >= 1:
                    dve.wait_ge(rot_made, n + dyn)
                nc.vector.tensor_tensor(rot_c, source, cos_t[:, :, :], ALU.mult).then_inc(rot_step, 1)
                nc.vector.tensor_tensor(rot_s, source, sin_t[:, :, :], ALU.mult).then_inc(rot_step, 1)

            def rotate_end(n, dyn=0):
                dve.wait_ge(rot_step, 2 * n + 2 + 2 * dyn)
                nc.vector.tensor_tensor(rot_x[:, 0, :], rot_c[:, 0, :], rot_s[:, 1, :], ALU.subtract)
                nc.vector.tensor_tensor(rot_x[:, 1, :], rot_c[:, 1, :], rot_s[:, 0, :],
                                        ALU.add).then_inc(rot_made, 1)

            def rotated_low(n, dst, dyn=0):
                dve.wait_ge(rot_hi, n + 1 + dyn)
                nc.vector.tensor_tensor(dst[:, :, SEQ:2 * SEQ], rot_x, as_f32(dst[:, :, 0:SEQ]),
                                        ALU.subtract).then_inc(rotated, 1)

            def fold_sum(n, dyn, low, summed, side):
                dve.wait_ge(low, n + 1 + dyn)
                nc.vector.tensor_tensor(fold_s[side], ps[:, 4 * side:4 * side + 4, 0:SEQ], fold_b[side],
                                        ALU.add).then_inc(summed, 1)

            def k_sum(g, dyn=0):
                for half in range(2):
                    dve.wait_ge(k_low, 2 * g + half + 1 + 2 * dyn)
                    b = slice(2 * half, 2 * half + 2)
                    nc.vector.tensor_tensor(fold_s[1][:, b, :], ps[:, 4 + 2 * half:6 + 2 * half, 0:SEQ],
                                            fold_b[1][:, b, :], ALU.add).then_inc(k_summed, 1)

            def subtract_hi(n, dyn, value, dst, hi, made):
                dve.wait_ge(hi, n + 1 + dyn)
                nc.vector.tensor_tensor(dst[:, :, SEQ:2 * SEQ], value, as_f32(dst[:, :, 0:SEQ]),
                                        ALU.subtract).then_inc(made, 1)

            def r_sum(g, dyn=0):
                dve.wait_ge(rot_low, g + 1 + dyn)
                bank = 0 if g == 0 else 4
                nc.vector.tensor_tensor(rot_x, ps[:, bank:bank + 2, 0:SEQ], rot_b, ALU.add).then_inc(r_summed, 1)
                dve.wait_ge(r_summed, g + 1 + dyn)

            def v_low(g, dyn=0):
                dve.wait_ge(v_hi_made, g + 1 + dyn)
                nc.vector.tensor_tensor(v_lo[:, :, :], ps[:, 6:8, :], as_f32(v_hi[:, :, :]),
                                        ALU.subtract).then_inc(v_made, 1)

            def mask_scores(g, dyn=0):
                for h in range(GH):
                    if h % 2 == 0:
                        dve.wait_ge(scores_done, 2 * g + h // 2 + 1 + dyn * 2)
                        nc.vector.memset(step_mark[:, h // 2:h // 2 + 1], 0.0)
                    for t in range(NT):
                        lo, hi = SCORE_COLS[t]
                        i = NT * h + t
                        nc.vector.tensor_tensor_reduce(
                            out=probs[:, h, lo:hi], in0=ps[:, 4 + h, lo:hi], in1=causal[:, (1 - t) * P:2 * P],
                            scale=1.0, scalar=-3.4e38, op0=ALU.add, op1=ALU.max,
                            accum_out=row_max[:, i:i + 1]).then_inc(scores_masked, 1)
                dve.wait_ge(scores_masked, 8 * (g + 1) + dyn * 8)
                nc.vector.tensor_scalar(neg_max, row_max, -SCALE, None, ALU.mult).then_inc(neg_max_made, 1)

            def normalise(g, dyn=0):
                dve.wait_ge(exp_made, 8 * (g + 1) + dyn * 8)
                nc.vector.reciprocal(inv_sum, row_sum).then_inc(inv_made, 1)
                dve.wait_ge(inv_made, g + 1 + dyn)
                for h in range(GH):
                    for t in range(NT):
                        i = NT * h + t
                        part = probs[:, h, SCORE_COLS[t][0]:SCORE_COLS[t][1]]
                        nc.vector.tensor_scalar(part, part, inv_sum[:, i:i + 1], None, ALU.mult).then_inc(probs_made, 1)

            def pt_low(g, dyn=0):
                dve.wait_ge(pt_hi_made, 2 * (g + 1) + dyn * 2)
                nc.vector.tensor_tensor(p_t[:, :, 2 * P:4 * P], ps[:, 0:4, 0:2 * P], as_f32(p_t[:, :, 0:2 * P]),
                                        ALU.subtract).then_inc(pt_made, 1)
                nc.vector.tensor_tensor(p_t[:, :, 5 * P:6 * P], ps[:, 0:4, 2 * P:3 * P],
                                        as_f32(p_t[:, :, 4 * P:5 * P]), ALU.subtract).then_inc(pt_made, 1)

            def o_low_part(g, dyn=0):
                dve.wait_ge(o_hi, g + 1 + dyn)
                heads = xt[:, bass.ds(dyn * GH + g * GH, GH), :]
                nc.vector.tensor_tensor(heads[:, :, SEQ:2 * SEQ], fold_s[0], as_f32(heads[:, :, 0:SEQ]),
                                        ALU.subtract).then_inc(o_made, 1)

            def attention_step(g, i=0):
                b, dyn = U_ATT + 8 * (g + 1), i * 8
                if g >= 0:
                    mask_scores(g, i)
                position(b, dyn)
                fold_sum(g + 1, i, q_low, q_summed, 0)
                if g >= 0:
                    normalise(g, i)
                position(b + 1, dyn)
                subtract_hi(g + 1, i, fold_s[0], q_t, q_hi, q_made)
                k_sum(g + 1, i)
                position(b + 2, dyn)
                if g >= 0:
                    pt_low(g, i)
                    position(b + 3, dyn)
                subtract_hi(g + 1, i, fold_s[1], k_t, k_hi, k_made)
                r_sum(g + 1, i)
                if g < 0:
                    position(b + 3)
                rotate_start(g + 2, rot_x, i)
                if g >= 0:
                    position(b + 4, dyn)
                rotate_end(g + 2, i)
                if g >= 0:
                    position(b + 5, dyn)
                rotated_low(g + 2, qr_t, i)
                if g >= 0:
                    fold_sum(g, i, o_low, o_summed, 0)
                else:
                    position(b + 4)
                    position(b + 5)
                position(b + 6, dyn)
                v_low(g + 1, i)
                if g >= 0:
                    o_low_part(g, i)
                position(b + 7, dyn)

            def add_slab(k, s, n, bank, scale=None, dyn=0, s_dyn=0):
                dve.wait_ge(unit_used, k + 1 + dyn)
                if s >= 1:
                    dve.wait_ge(slab_read, s + s_dyn)
                for t in range(NT):
                    cols = resid[:, t, n * COLS:(n + 1) * COLS]
                    sums = ps[:, bank + 2 * (n % 2) + t, :]
                    if scale is None:
                        last = nc.vector.tensor_tensor(cols, sums, cols, ALU.add)
                    else:
                        last = nc.vector.scalar_tensor_tensor(out=cols, in0=sums, scalar=scale[:, t:t + 1],
                                                              in1=cols, op0=ALU.mult, op1=ALU.add)
                    if s == S_END - 1:
                        last.then_inc(last_added, 1)
                if s < S_END - 1:
                    last.then_inc(slab_read, 1)

            nc.vector.memset(eps, EPS).then_inc(eps_set, 1)
            rope_angles()
            for s in range(SLABS):
                if s == 0:
                    dve.wait_ge(gains_ready, 1)
                turn_lo(0, s)
                split(2 * s)
                split(2 * s + 1)
            make_rstd(0, 0)
            for k in range(U_DQKV + 4, U_ATT):
                if k == U_ATT - 1:
                    c_norm_factor(1)
                position(k)
                if k == 7:
                    dve.wait_ge(rstd_made, 1)
                    c_norm_factor(0)
                if k == 8:
                    dve.wait_ge(tail_hi_made, 1)
                    nc.vector.tensor_tensor(tail_lo, tail_raw, as_f32(tail_hi), ALU.subtract).then_inc(tail_made, 1)
                if k == 10:
                    dve.wait_ge(tables_made, 4)
                    dve.wait_ge(kr_low_made, 1)
                    nc.vector.tensor_tensor(kr_sum, ps[0:ROPE, 2, 0:SEQ], kr_low, ALU.add).then_inc(kr_summed, 1)
                if k == 11:
                    c_low(0)
                if k == 13:
                    dve.wait_ge(kr_turned, 1)
                    rotate_start(0, ps[:, 2, :].rearrange("p (a n) -> p a n", a=2))
            c_low(1)
            rotate_end(0)
            rotated_low(0, kr_t)
            attention_step(-1)
            with dve.Fori(0, GROUPS - 2) as i:
                attention_step(0, i)
            attention_step(GROUPS - 2)
            mask_scores(GROUPS - 1)
            normalise(GROUPS - 1)
            for k in range(U_WO, U_WO + 3):
                position(k)
            pt_low(GROUPS - 1)
            position(U_WO + 3)
            fold_sum(GROUPS - 1, 0, o_low, o_summed, 0)
            o_low_part(GROUPS - 1)

            for n in range(SLABS):
                for k in range(4 if n == 0 else 0, 8):
                    position(U_WO + 8 * n + k)
                    if n >= 1 and k == 3:
                        turn_lo(1, n - 1)
                add_slab(U_WO + 8 * n + 7, S_WO + n, n, 4)

            def mlp(layer, norm_index):
                s0 = layer * FF_SLABS

                def up(b, s, dyn=0, s_dyn=0):
                    side = 0 if s == 0 else 1
                    for k in range(8):
                        position(b + k, dyn)
                        if s == 0 and k == 1:
                            turn_lo(norm_index, SLABS - 1)
                        if s == 0 and k == 4:
                            make_rstd_sq(layer, norm_index)
                    dve.wait_ge(up_low, s0 + s + 1 + s_dyn)
                    nc.vector.tensor_tensor(fold_s[0], ps[:, 4 * side:4 * side + 4, 0:SEQ], fold_b[0],
                                            ALU.add).then_inc(up_summed, 1)

                def square(s, s_dyn=0):
                    dve.wait_ge(up_summed, s0 + s + 1 + s_dyn)
                    nc.vector.scalar_tensor_tensor(out=fold_s[1], in0=fold_s[0], scalar=0.0, in1=fold_s[0],
                                                   op0=ALU.max, op1=ALU.mult).then_inc(up_squared, 1)

                def square_low(s, s_dyn=0):
                    subtract_hi(s0 + s, s_dyn, fold_s[1], mid[:, s % 2, :, :], up_hi, up_made)

                def down(b, s, s_up, dyn=0, s_dyn=0):
                    for k in range(8):
                        position(b + k, dyn)
                        if s_up is not None and k == 0:
                            square(s_up, s_dyn)
                        if s_up is not None and k == 2:
                            square_low(s_up, s_dyn)
                        if k % 2 == 1:
                            add_slab(b + k, S_MLP[layer] + s * SLABS + k // 2, k // 2, 0, rstd_sq, dyn,
                                     s_dyn * SLABS)
                        if s_up is None and k % 2 == 1 and k > 1 and layer == 0:
                            turn_lo(norm_index + 1, k // 2 - 1)

                b = U_MLP[layer]
                up(b, 0)
                square(0)
                square_low(0)
                with dve.Fori(0, FF_SLABS // 2 - 1) as i:
                    up(b + 8, 1, i * 32, i * 2)
                    down(b + 16, 0, 1, i * 32, i * 2)
                    up(b + 24, 2, i * 32, i * 2)
                    down(b + 32, 1, 2, i * 32, i * 2)
                b = U_MLP[layer] + 16 * FF_SLABS - 24
                up(b, FF_SLABS - 1)
                down(b + 8, FF_SLABS - 2, FF_SLABS - 1)
                down(b + 16, FF_SLABS - 1, None)

            def scale_products(g):
                dve.wait_ge(unit_used, U_POOL + 2 * g + 2)
                if g >= 2:
                    dve.wait_ge(pooled, g - 1)
                for t in range(NT):
                    nc.vector.tensor_tensor(pool_sums[g % 2][:, t, :], ps[:, 2 * (g % 2) + t, :],
                                            row_gain[:, g * COLS:(g + 1) * COLS], ALU.mult).then_inc(pool_scaled, 1)

            def add_pooled(g):
                dve.wait_ge(pooled, g + 1)
                dve.wait_ge(slab_read, S_POOL)
                cols, sums = slice(g * COLS, (g + 1) * COLS), ps[:, 4 + 2 * (g % 2):6 + 2 * (g % 2), :]
                nc.vector.tensor_tensor(resid[:, :, cols], sums, resid[:, :, cols], ALU.add).then_inc(slab_read, 1)

            mlp(0, 1)
            dve.wait_ge(band_in, 16)
            dve.wait_ge(scale_in, 16)
            make_rstd(1, 2)
            dve.wait_ge(rstd_made, 2)
            for t, cols in ((0, slice(0, SEQ)), (1, slice(SEQ, SEQ + P))):
                nc.vector.tensor_scalar(bands[:, :, cols], bands[:, :, cols], rstd[:, t:t + 1], None,
                                        ALU.mult).then_inc(bands_scaled, 1)
            for k in range(U_POOL, U_MLP[1]):
                position(k)
                if k % 2 == 1:
                    scale_products((k - U_POOL) // 2)
                if k == U_POOL + 1:
                    turn_lo(2, SLABS - 1)
                if k > U_POOL + 3 and k % 2 == 1:
                    add_pooled((k - U_POOL) // 2 - 2)
            turn_lo(3, 0)
            add_pooled(SLABS - 2)
            turn_lo(3, 1)
            add_pooled(SLABS - 1)
            turn_lo(3, 2)
            mlp(1, 3)
            dve.wait_ge(final_in, 16)
            for t in range(NT):
                dve.wait_ge(last_added, t + 1)
                nc.vector.tensor_tensor(last_gained[:, t, :], resid[:, t, LAST_COLS], row_gain[:, LAST_COLS],
                                        ALU.mult).then_inc(gained, 1)
            make_rstd(2, 4)
            dve.wait_ge(rstd_made, 3)
            dve.wait_ge(gained, NT * SLABS)
            for s in range(SLABS):
                nc.vector.tensor_scalar(result[:, 1, s * COLS:(s + 1) * COLS], gained_slab(s, 1), rstd[:, 1:2], None,
                                        ALU.mult).then_inc(final_t1, 1)

        @block.tensor
        def _(pe):
            mm = nc.tensor.matmul

            def token_unit(k, source, tile, bank, first, last, dyn=0):
                pe.wait_ge(lo_made, k + 1 + dyn)
                s = k % LEAD
                for j in range(2):
                    for t in range(NT):
                        hi = source[:, tile + j, t * P:(t + 1) * P]
                        lo = source[:, tile + j, SEQ + t * P:SEQ + (t + 1) * P]
                        o = ps[:, bank + t, :]
                        mm(o, hi, weight_hi[:, s, j, :], start=first and j == 0, stop=False)
                        mm(o, hi, weight_lo[:, s, j, :], start=False, stop=False)
                        end = mm(o, lo, weight_hi[:, s, j, :], start=False, stop=last and j == 1)
                end.then_inc(unit_used, 1)

            def weight_unit(k, source, tile, bank, first, last, dyn=0, blocks=FB):
                pe.wait_ge(lo_made, k + 1 + dyn)
                s = k % LEAD
                for j in range(2):
                    for f in range(blocks):
                        w_hi = weight_hi[:, s, j, f * P:(f + 1) * P]
                        w_lo = weight_lo[:, s, j, f * P:(f + 1) * P]
                        both = (w_hi, source[:, tile + j, :], ps[:, bank + f, :])
                        high = (w_lo, source[:, tile + j, 0:SEQ], ps[:, bank + f, 0:SEQ])
                        order = (high, both) if j == 1 else (both, high)
                        for i, (w, m, o) in enumerate(order):
                            end = mm(o, w, m, start=first and j == 0 and i == 0, stop=last and j == 1 and i == 1)
                end.then_inc(unit_used, 1)

            def turn(n, s):
                if n == 0:
                    pe.wait_ge(x_in[s], 16)
                else:
                    pe.wait_ge(slab_read, ADDED_BEFORE[n] + s + 1)
                if s == 2 and TURN_BANK[n][s] == TURN_BANK[n][0]:
                    xt_ready(n, 3)
                if n == 2 and s == 3:
                    xt_ready(n, 7)
                for b in range(2):
                    for a in range(2):
                        f = s * COLS + (2 * b + a) * P
                        for t in range(NT):
                            end = nc.tensor.transpose(
                                ps[:, TURN_BANK[n][s] + b, a * SEQ + t * P:a * SEQ + (t + 1) * P],
                                resid[:, t, f:f + P], ident)
                    end.then_inc(turned, 1)

            def xt_ready(n, k):
                pe.wait_ge(xt_made, KT * n + k + 1)

            def c_turn(j):
                pe.wait_ge(c_scaled, NT * (j + 1))
                for b in range(2):
                    for a in range(2):
                        for t in range(NT):
                            f = j * LORA + (2 * b + a) * P
                            end = nc.tensor.transpose(ps[:, 6 * j + b, a * SEQ + t * P:a * SEQ + (t + 1) * P],
                                                      latent[:, t, f:f + P], ident)
                    end.then_inc(c_turned, 1)

            pe.wait_ge(consts_in, 16)
            turn(0, 0)
            pe.wait_ge(gains_in, 64)
            nc.tensor.transpose(ps[:, 7, 0:N_GAINS], gain_rows, ident[0:N_GAINS, 0:N_GAINS]).then_inc(gains_turned, 1)
            for slab in range(2):
                for u in range(8):
                    if slab == 0:
                        if u in (0, 2, 4):
                            turn(0, u // 2 + 1)
                        xt_ready(0, 2 * u + 1)
                    token_unit(U_DQKV + 8 * slab + u, xt, 2 * u, 4 + 2 * slab, u == 0, u == 7)
                    if slab == 1 and u == 2:
                        pe.wait_ge(tail_made, 1)
                        for k in range(KT):
                            mm(ps[0:ROPE, 2, :], tail_hi[:, k, :], xt[:, k, :], start=k == 0, stop=False)
                            end = mm(ps[0:ROPE, 2, 0:SEQ], tail_lo[:, k, :], xt[:, k, 0:SEQ],
                                     start=False, stop=k == KT - 1)
                        end.then_inc(tail_done, 1)
                    if slab == 1 and u == 3:
                        c_turn(0)
                    if slab == 1 and u == 4:
                        pe.wait_ge(kr_summed, 1)
                        for t in range(NT):
                            end = nc.tensor.transpose(ps[:, 3, t * ROPE:(t + 1) * ROPE],
                                                      kr_sum[:, t * P:(t + 1) * P], ident[0:ROPE, 0:ROPE])
                        end.then_inc(kr_back, 1)
                    if slab == 1 and u == 5:
                        pe.wait_ge(kr_copied, 1)
                        for a in range(2):
                            for t in range(NT):
                                end = nc.tensor.transpose(
                                    ps[:, 2, a * SEQ + t * P:a * SEQ + (t + 1) * P],
                                    k_rope[:, t, a, :, :].rearrange("p r j -> p (r j)"), ident)
                        end.then_inc(kr_turned, 1)
            pe.wait_ge(ct_made, LT)
            pe.wait_ge(rot_step, 2)

            def project_q(g, i=0, units=(0, 1)):
                b = U_ATT + 8 * g
                for u in units:
                    weight_unit(b + u, latent_t, 2 * u, 0, u == 0, u == 1, i * 8)

            project_q(0, units=(0,))
            c_turn(1)
            project_q(0, units=(1,))

            def project_k(g, i=0):
                b = U_ATT + 8 * g + 2
                for u in range(2):
                    weight_unit(b + u, latent_t, LT + 2 * u, 4, u == 0, u == 1, i * 8)

            def project_rope(g, i=0, bank=4):
                b = U_ATT + 8 * g + 4
                for u in range(2):
                    weight_unit(b + u, latent_t, 2 * u, bank, u == 0, u == 1, i * 8, blocks=2)

            def project_v(g, i=0):
                b = U_ATT + 8 * g + 6
                for u in range(2):
                    token_unit(b + u, latent_t, LT + 2 * u, 6, u == 0, u == 1, i * 8)

            def scores(g, i=0):
                pe.wait_ge(q_made, g + 1 + i)
                pe.wait_ge(k_made, g + 1 + i)
                pe.wait_ge(rotated, g + 2 + i)
                for h in range(GH):
                    if h == 2:
                        pe.wait_ge(v_made, g + 1 + i)
                    for t in range(NT):
                        lo, hi = SCORE_COLS[t]
                        o, keys = ps[:, 4 + h, lo:hi], (t + 1) * P

                        def three(rows, q, k, start, stop):
                            q_hi, q_lo = q[rows, t * P:(t + 1) * P], q[rows, SEQ + t * P:SEQ + (t + 1) * P]
                            k_hi, k_lo = k[rows, 0:keys], k[rows, SEQ:SEQ + keys]
                            mm(o, q_hi, k_hi, start=start, stop=False)
                            mm(o, q_hi, k_lo, start=False, stop=False)
                            return mm(o, q_lo, k_hi, start=False, stop=stop)

                        three(slice(0, P), q_t[:, h, :], k_t[:, h, :], True, False)
                        rows = slice(h * HALF, (h + 1) * HALF)
                        three(rows, qr_t[:, 0, :], kr_t[:, 0, :], False, False)
                        end = three(rows, qr_t[:, 1, :], kr_t[:, 1, :], False, True)
                    if h % 2 == 1:
                        end.then_inc(scores_done, 1)

            def turn_probs(g, i=0):
                pe.wait_ge(probs_made, 8 * (g + 1) + i * 8)
                pe.wait_ge(q_summed, min(g + 2, GROUPS) + i)
                for h in range(GH):
                    for c in (0, P, 2 * P):
                        end = nc.tensor.transpose(ps[:, h, c:c + P], probs[:, h, c:c + P], ident)
                end.then_inc(probs_turned, 1)

            def values(g, i=0):
                pe.wait_ge(pt_made, 2 * (g + 1) + i * 2)
                pe.wait_ge(v_made, g + 1 + i)
                for h in range(GH):
                    c = slice(h * V_HEAD, (h + 1) * V_HEAD)
                    halves = ps[:, h, :].rearrange("p (a n) -> p a n", a=2)
                    mm(ps[:, h, :], v_hi[:, 0, c], p_t[:, h, 0:4 * P], start=True, stop=False)
                    mm(ps[:, h, 0:SEQ], v_lo[:, 0, c], p_t[:, h, 0:2 * P], start=False, stop=False)
                    mm(ps[:, h, P:SEQ], v_lo[:, 1, c], p_t[:, h, 4 * P:5 * P], start=False, stop=False)
                    end = mm(halves[:, :, P:2 * P], v_hi[:, 1, c],
                             p_t[:, h, 4 * P:6 * P].rearrange("p (a n) -> p a n", a=2), start=False, stop=True)
                end.then_inc(o_done, 1)

            def attention_step(g, i=0):
                scores(g, i)
                if g > 0:
                    pe.wait_ge(o_summed, g + i)
                else:
                    pe.wait_ge(r_summed, 1)
                project_q(g + 1, i)
                pe.wait_ge(scores_masked, 8 * (g + 1) + i * 8)
                project_k(g + 1, i)
                turn_probs(g, i)
                pe.wait_ge(k_summed, 2 * g + 3 + 2 * i)
                project_rope(g + 1, i)
                values(g, i)
                pe.wait_ge(k_summed, 2 * g + 4 + 2 * i)
                project_v(g + 1, i)

            def project_out(n, u):
                token_unit(U_WO + 8 * n + u, xt, 2 * u, 4 + 2 * (n % 2), u == 0, u == 7)

            pe.wait_ge(ct_made, 2 * LT)
            project_k(0)
            pe.wait_ge(q_summed, 1)
            project_rope(0, bank=0)
            pe.wait_ge(k_summed, 2)
            project_v(0)
            attention_step(0)
            with pe.Fori(0, GROUPS - 2) as i:
                attention_step(1, i)
            scores(GROUPS - 1)
            pe.wait_ge(scores_masked, 8 * GROUPS - 4)
            pe.wait_ge(o_made, GROUPS - 1)
            for u in range(3):
                project_out(0, u)
            turn_probs(GROUPS - 1)
            project_out(0, 3)
            values(GROUPS - 1)
            project_out(0, 4)
            project_out(0, 5)
            pe.wait_ge(o_made, GROUPS)
            for n in range(SLABS):
                if n >= 2:
                    pe.wait_ge(slab_read, S_WO + n - 1)
                for u in range(6 if n == 0 else 0, 8):
                    project_out(n, u)
                    if n >= 1 and u == 3:
                        turn(1, n - 1)

            def mlp(layer, norm_index):
                s0 = layer * FF_SLABS

                def up(b, s, dyn=0, s_dyn=0):
                    if s >= 2:
                        pe.wait_ge(up_summed, s0 + s + s_dyn)
                    for u in range(8):
                        if s == 0:
                            xt_ready(norm_index, max(2 * u + 1, 7))
                        weight_unit(b + u, xt2, 2 * u, 0 if s == 0 else 4, u == 0, u == 7, dyn)
                        if s == 0 and u == 1:
                            turn(norm_index, SLABS - 1)

                def down(b, s, dyn=0, s_dyn=0, closing=False):
                    pe.wait_ge(up_made, s0 + s + 1 + s_dyn)
                    for n in range(SLABS):
                        pe.wait_ge(slab_read, S_MLP[layer] + s * SLABS + n - 1 + s_dyn * SLABS)
                        for u in range(2):
                            token_unit(b + 2 * n + u, mid[:, s % 2, :, :], 2 * u, 2 * (n % 2),
                                       u == 0, u == 1, dyn)
                        if closing and n >= 1:
                            turn(2, n - 1)

                b = U_MLP[layer]
                up(b, 0)
                up(b + 8, 1)
                down(b + 16, 0)
                up(b + 24, 2)
                down(b + 32, 1)
                b += 32
                with pe.Fori(0, FF_SLABS // 2 - 2) as i:
                    up(b + 8, 3, i * 32, i * 2)
                    down(b + 16, 2, i * 32, i * 2)
                    up(b + 24, 4, i * 32, i * 2)
                    down(b + 32, 3, i * 32, i * 2)
                b = U_MLP[layer] + 16 * FF_SLABS - 24
                up(b, FF_SLABS - 1)
                down(b + 8, FF_SLABS - 2)
                down(b + 16, FF_SLABS - 1, closing=layer == 0)

            def pool_products(g):
                xt_ready(2, LT * g + LT - 1)
                if g < 2:
                    pe.wait_ge(slab_read, S_POOL - 1 + g)
                else:
                    pe.wait_ge(pool_scaled, NT * (g - 1))
                for u in range(2):
                    token_unit(U_POOL + 2 * g + u, xt, LT * g + 2 * u, 2 * (g % 2), u == 0, u == 1)

            def pool_windows(g):
                pe.wait_ge(pool_scaled, NT * (g + 1))
                if g == 0:
                    pe.wait_ge(bands_scaled, NT)
                    xt_ready(2, KT - 1)
                if g >= 2:
                    pe.wait_ge(slab_read, S_POOL + g - 1)
                o, z = 4 + 2 * (g % 2), pool_sums[g % 2]
                mm(ps[:, o, :], bands[:, g, 0:P], z[:, 0, :], start=True, stop=True)
                mm(ps[:, o + 1, :], bands[:, g, P:2 * P], z[:, 0, :], start=True, stop=False)
                mm(ps[:, o + 1, :], bands[:, g, 2 * P:3 * P], z[:, 1, :], start=False, stop=True).then_inc(pooled, 1)

            mlp(0, 1)
            pool_products(0)
            pool_products(1)
            turn(2, SLABS - 1)
            pool_products(2)
            pool_windows(0)
            pool_products(3)
            pool_windows(1)
            pe.wait_ge(pool_scaled, NT * 3)
            turn(3, 0)
            pool_windows(2)
            pe.wait_ge(pool_scaled, NT * 4)
            turn(3, 1)
            pool_windows(3)
            turn(3, 2)
            mlp(1, 3)


_INS = ["x", "positions", "ln_mix", "ln_mlp", "w_dqkv", "q_norm", "kv_norm", "w_uq", "w_ukv", "w_o",
        "w_pool", "pool_scale", "w_up", "w_down", "final_norm"]


def shape_constants():
    causal = np.zeros((P, 2 * P), np.float32)
    causal[:, P:] = np.where(np.arange(P)[None, :] <= np.arange(P)[:, None], 0.0, MASKED)
    exponent = np.arange(0, ROPE, 2, dtype=np.float32) / np.float32(ROPE)
    inv_freq = (np.float32(1.0) / np.power(np.float32(ROPE_THETA), exponent)).astype(np.float32)
    first = np.concatenate([np.eye(P, dtype=np.float32), causal, np.tile(inv_freq, P // HALF)[:, None]], axis=1)
    s, t = np.arange(SEQ)[:, None], np.arange(SEQ)[None, :]
    bands = []
    for w in WINDOWS:
        inside = (s <= t) & (s > t - w)
        bands.append((inside / np.minimum(t + 1, w) - (s == t)).astype(np.float32))
    second = np.concatenate([np.concatenate([b[0:P, :], b[P:, P:]], axis=1) for b in bands], axis=1)
    return np.ascontiguousarray(first), np.ascontiguousarray(second)


def kernel(**inputs):
    import concourse.bacc as _bacc
    from concourse.bass_utils import run_bass_kernel_spmd as _run

    nc = _bacc.Bacc("TRN2", target_bir_lowering=False, num_devices=1, dynamic_dma_scratch_size=8192)
    arrays, args = {}, []
    consts, bands = shape_constants()
    given = [(name, np.ascontiguousarray(inputs[name])) for name in _INS]
    for name, a in given + [("shape_consts", consts), ("band_consts", bands)]:
        arrays[f"in_{name}"] = a
        args.append(nc.dram_tensor(f"in_{name}", a.shape, mybir.dt.from_np(a.dtype), kind="ExternalInput").ap())
    args.append(nc.dram_tensor("out_0", (1, SEQ, D_MODEL), F32, kind="ExternalOutput").ap())
    trunk(nc, *args)
    r = _run(nc, [arrays], core_ids=[0])
    return r.results[0]["out_0"]
```
